# Optimizing a Trainium2 kernel written in Bass

```python
import math
import jax, jax.numpy as jnp
from jax import lax
import numpy as np

D_MODEL = 1024
BATCH = 1
SEQ = 128
DEPTH = 2
DEC_BATCH = 1
DEC_SEQ = 256
PAST_LEN = 128

GRID_W = 64
Q_BLOCK = 128
HD = 64
A_HEADS = 6
A_KV = 2
A_WIDTH = A_HEADS * HD
B_HEADS = 6
B_DK = 32
B_WIDTH = B_HEADS * 2 * B_DK
C_WIDTH = 256
D_MIX = A_WIDTH + B_WIDTH + C_WIDTH
SPLITS = (A_HEADS * HD, A_KV * HD, A_KV * HD,
          B_HEADS * 2 * B_DK, B_HEADS * 2 * B_DK, B_WIDTH,
          C_WIDTH, C_WIDTH, C_WIDTH)
D_PROJ = 640 + 1152 + 768
ROPE_BASE = 10000.0
EPS = 1e-6
P_HEADS = 8
N_KEYS = 128
N_EXPERTS = N_KEYS * N_KEYS
P_QDIM = 256
P_HALF = P_QDIM // 2
P_TOPK = 16
P_CHUNK = 128

kernel_name = "hymba_diffusion_peer_step"

def rms_norm(x, g):
    xf = x.astype(jnp.float32)
    y = xf * lax.rsqrt(jnp.mean(xf * xf, axis=-1, keepdims=True) + EPS)
    return y.astype(x.dtype) * g

def axial_rope_tables(n_tokens, dim):
    n_rows = n_tokens // GRID_W
    row = jnp.broadcast_to(jnp.arange(n_rows)[:, None], (n_rows, GRID_W)).reshape(-1)
    col = jnp.broadcast_to(jnp.arange(GRID_W)[None, :], (n_rows, GRID_W)).reshape(-1)
    quarter = dim // 4
    inv = ROPE_BASE ** (-jnp.arange(quarter, dtype=jnp.float32) / quarter)
    ang_r = row.astype(jnp.float32)[:, None] * inv
    ang_c = col.astype(jnp.float32)[:, None] * inv
    return (jnp.cos(ang_r), jnp.sin(ang_r), jnp.cos(ang_c), jnp.sin(ang_c))

def _rotate(x, cos, sin):
    x1, x2 = jnp.split(x, 2, axis=-1)
    return jnp.concatenate([x1 * cos - x2 * sin, x2 * cos + x1 * sin], axis=-1)

def apply_axial_rope(x, tables):
    cr, sr, cc, sc = tables
    extra = x.ndim - 3
    shp = lambda t: t.reshape(t.shape[:1] + (1,) * extra + t.shape[1:]).astype(x.dtype)
    xr, xc = jnp.split(x, 2, axis=-1)
    return jnp.concatenate([_rotate(xr, shp(cr), shp(sr)), _rotate(xc, shp(cc), shp(sc))], axis=-1)

def gqa_attention(q, k, v):
    b, s, h, d = q.shape
    kv = k.shape[2]
    g = h // kv
    nb = s // Q_BLOCK
    qb = q.reshape(b, nb, Q_BLOCK, kv, g, d).transpose(1, 0, 2, 3, 4, 5)
    scale = d ** -0.5

    def one_block(qblk):
        sc = jnp.einsum('bqkgd,blkd->bkgql', qblk, k).astype(jnp.float32) * scale
        p = jax.nn.softmax(sc, axis=-1).astype(v.dtype)
        return jnp.einsum('bkgql,blkd->bqkgd', p, v)

    o = lax.map(one_block, qb)
    return o.transpose(1, 0, 2, 3, 4, 5).reshape(b, s, h * d)

def diff_attention(q, k, v, lam):
    b, s, h, _, dk = q.shape
    nb = s // Q_BLOCK
    qb = q.reshape(b, nb, Q_BLOCK, h, 2, dk).transpose(1, 0, 2, 3, 4, 5)
    scale = dk ** -0.5

    def one_block(qblk):
        sc = jnp.einsum('bqhjd,blhjd->bhjql', qblk, k).astype(jnp.float32) * scale
        p = jax.nn.softmax(sc, axis=-1)
        a = (p[:, :, 0] - lam * p[:, :, 1]).astype(v.dtype)
        return jnp.einsum('bhql,blhe->bqhe', a, v)

    o = lax.map(one_block, qb)
    return o.transpose(1, 0, 2, 3, 4).reshape(b, s, h, v.shape[-1])

def short_conv_mixer(x_in, b_gate, c_gate, w, bias):
    u = c_gate * x_in
    s = u.shape[1]
    up = jnp.pad(u, ((0, 0), (1, 1), (0, 0)))
    y = up[:, :s] * w[0] + up[:, 1:s + 1] * w[1] + up[:, 2:] * w[2] + bias
    return b_gate * y

def peer_ffn(h, wq, sub_keys, u_tab, v_tab):
    b, s, d = h.shape
    x = h.reshape(-1, P_CHUNK, d)

    def one_chunk(xc):
        q = (xc @ wq).reshape(P_CHUNK, P_HEADS, 2, P_HALF)
        sc = jnp.einsum('thcd,hcnd->thcn', q, sub_keys).astype(jnp.float32)
        s1, i1 = lax.top_k(sc[:, :, 0], P_TOPK)
        s2, i2 = lax.top_k(sc[:, :, 1], P_TOPK)
        cand = (s1[..., :, None] + s2[..., None, :]).reshape(P_CHUNK, P_HEADS, P_TOPK * P_TOPK)
        cand_idx = (i1[..., :, None] * N_KEYS + i2[..., None, :]).reshape(P_CHUNK, P_HEADS, P_TOPK * P_TOPK)
        top_s, pos = lax.top_k(cand, P_TOPK)
        eidx = jnp.take_along_axis(cand_idx, pos, axis=-1)
        gate = jax.nn.softmax(top_s, axis=-1).astype(xc.dtype)
        u = jnp.take(u_tab, eidx, axis=0)
        act = jax.nn.gelu(jnp.einsum('thkd,td->thk', u, xc))
        vv = jnp.take(v_tab, eidx, axis=0)
        return jnp.einsum('thk,thkd->td', gate * act, vv)

    return lax.map(one_chunk, x).reshape(b, s, d)

def modulation(cond, ada_w, ada_b):
    m = jax.nn.silu(cond) @ ada_w + ada_b
    return jnp.split(m[:, None, :], 6, axis=-1)

def split_projection(h, w_in, qn_a, kn_a, qn_b, kn_b):
    b, s, _ = h.shape
    p = h @ w_in
    offsets = np.cumsum(np.array(SPLITS))[:-1].tolist()
    qa, ka, va, qb, kb, vb, ci, cb, cc = jnp.split(p, offsets, axis=-1)
    qa = rms_norm(qa.reshape(b, s, A_HEADS, HD), qn_a)
    ka = rms_norm(ka.reshape(b, s, A_KV, HD), kn_a)
    va = va.reshape(b, s, A_KV, HD)
    qb = rms_norm(qb.reshape(b, s, B_HEADS, 2, B_DK), qn_b)
    kb = rms_norm(kb.reshape(b, s, B_HEADS, 2, B_DK), kn_b)
    vb = vb.reshape(b, s, B_HEADS, 2 * B_DK)
    return qa, ka, va, qb, kb, vb, ci, cb, cc

def merge_mixers(oa, ob, oc, lam_init, subln_g, out_norm_a, out_norm_c, w_out):
    b, s = oa.shape[:2]
    ob = rms_norm(ob, subln_g) * (1.0 - lam_init)
    y = jnp.concatenate([rms_norm(oa, out_norm_a), ob.reshape(b, s, B_WIDTH),
                         rms_norm(oc, out_norm_c)], axis=-1)
    return y @ w_out

def setup_inputs(seed: int = 0) -> dict:
    key = jax.random.key(seed)
    ks = iter(jax.random.split(key, 40))
    nrm = lambda shape, scale=1.0: jax.random.normal(next(ks), shape, jnp.float32) * scale
    gain = lambda shape: 1.0 + 0.02 * jax.random.normal(next(ks), shape, jnp.float32)
    return {
        "x_prompt": nrm((BATCH, SEQ, D_MODEL)),
        "x_sample": nrm((DEC_BATCH, DEC_SEQ, D_MODEL)),
        "cache_a_k": nrm((DEC_BATCH, DEPTH, PAST_LEN, A_KV, HD)),
        "cache_a_v": nrm((DEC_BATCH, DEPTH, PAST_LEN, A_KV, HD)),
        "cache_b_k": nrm((DEC_BATCH, DEPTH, PAST_LEN, B_HEADS, 2, B_DK)),
        "cache_b_v": nrm((DEC_BATCH, DEPTH, PAST_LEN, B_HEADS, 2 * B_DK)),
        "c": nrm((DEC_BATCH, D_MODEL)),
        "c_ctx": nrm((D_MODEL,)),
        "ada_w": nrm((DEPTH, D_MODEL, 6 * D_MODEL), 0.5 * D_MODEL ** -0.5),
        "ada_b": nrm((DEPTH, 6 * D_MODEL), 0.02),
        "norm1_g": gain((DEPTH, D_MODEL)),
        "norm2_g": gain((DEPTH, D_MODEL)),
        "w_in": nrm((DEPTH, D_MODEL, D_PROJ), D_MODEL ** -0.5),
        "qn_a": gain((DEPTH, HD)),
        "kn_a": gain((DEPTH, HD)),
        "qn_b": gain((DEPTH, B_DK)),
        "kn_b": gain((DEPTH, B_DK)),
        "lam_q1": nrm((DEPTH, B_DK), 0.1),
        "lam_k1": nrm((DEPTH, B_DK), 0.1),
        "lam_q2": nrm((DEPTH, B_DK), 0.1),
        "lam_k2": nrm((DEPTH, B_DK), 0.1),
        "subln_g": gain((DEPTH, 2 * B_DK)),
        "out_norm_a": gain((DEPTH, A_WIDTH)),
        "out_norm_c": gain((DEPTH, C_WIDTH)),
        "conv_w": nrm((DEPTH, 3, C_WIDTH), 3 ** -0.5),
        "conv_b": nrm((DEPTH, C_WIDTH), 0.02),
        "w_out": nrm((DEPTH, D_MIX, D_MODEL), D_MIX ** -0.5),
        "peer_wq": nrm((DEPTH, D_MODEL, P_HEADS * P_QDIM), D_MODEL ** -0.5),
        "peer_keys": nrm((DEPTH, P_HEADS, 2, N_KEYS, P_HALF), P_HALF ** -0.5),
        "peer_u": nrm((DEPTH, N_EXPERTS, D_MODEL), D_MODEL ** -0.5),
        "peer_v": nrm((DEPTH, N_EXPERTS, D_MODEL), 1.0),
    }

def reference(x_prompt, x_sample, cache_a_k, cache_a_v, cache_b_k, cache_b_v, c, c_ctx,
              ada_w, ada_b, norm1_g, norm2_g, w_in, qn_a, kn_a, qn_b, kn_b,
              lam_q1, lam_k1, lam_q2, lam_k2, subln_g, out_norm_a, out_norm_c,
              conv_w, conv_b, w_out, peer_wq, peer_keys, peer_u, peer_v):
    n_lat = x_sample.shape[1]
    rope_a = axial_rope_tables(n_lat, HD)
    rope_b = axial_rope_tables(n_lat, B_DK)
    xp = x_prompt
    xs = x_sample
    new_ak, new_av, new_bk, new_bv = [], [], [], []
    for l in range(DEPTH):
        lam_init = 0.8 - 0.6 * math.exp(-0.3 * l)
        lam = (jnp.exp(jnp.sum((lam_q1[l] * lam_k1[l]).astype(jnp.float32)))
               - jnp.exp(jnp.sum((lam_q2[l] * lam_k2[l]).astype(jnp.float32))) + lam_init)

        sh1, sc1, g1, sh2, sc2, g2 = modulation(c_ctx[None, :], ada_w[l], ada_b[l])
        h = rms_norm(xp, norm1_g[l]) * (1.0 + sc1) + sh1
        qa, ka, va, qb, kb, vb, ci, cb, cc = split_projection(h, w_in[l], qn_a[l], kn_a[l], qn_b[l], kn_b[l])
        new_ak.append(ka)
        new_av.append(va)
        new_bk.append(kb)
        new_bv.append(vb)
        oa = gqa_attention(qa, ka, va)
        ob = diff_attention(qb, kb, vb, lam)
        oc = short_conv_mixer(ci, cb, cc, conv_w[l], conv_b[l])
        xp = xp + g1 * merge_mixers(oa, ob, oc, lam_init, subln_g[l], out_norm_a[l], out_norm_c[l], w_out[l])
        h = rms_norm(xp, norm2_g[l]) * (1.0 + sc2) + sh2
        xp = xp + g2 * peer_ffn(h, peer_wq[l], peer_keys[l], peer_u[l], peer_v[l])

        sh1, sc1, g1, sh2, sc2, g2 = modulation(c, ada_w[l], ada_b[l])
        h = rms_norm(xs, norm1_g[l]) * (1.0 + sc1) + sh1
        qa, ka, va, qb, kb, vb, ci, cb, cc = split_projection(h, w_in[l], qn_a[l], kn_a[l], qn_b[l], kn_b[l])
        qa = apply_axial_rope(qa, rope_a)
        ka = apply_axial_rope(ka, rope_a)
        qb = apply_axial_rope(qb, rope_b)
        kb = apply_axial_rope(kb, rope_b)
        ka_all = jnp.concatenate([ka, cache_a_k[:, l]], axis=1)
        va_all = jnp.concatenate([va, cache_a_v[:, l]], axis=1)
        kb_all = jnp.concatenate([kb, cache_b_k[:, l]], axis=1)
        vb_all = jnp.concatenate([vb, cache_b_v[:, l]], axis=1)
        oa = gqa_attention(qa, ka_all, va_all)
        ob = diff_attention(qb, kb_all, vb_all, lam)
        oc = short_conv_mixer(ci, cb, cc, conv_w[l], conv_b[l])
        xs = xs + g1 * merge_mixers(oa, ob, oc, lam_init, subln_g[l], out_norm_a[l], out_norm_c[l], w_out[l])
        h = rms_norm(xs, norm2_g[l]) * (1.0 + sc2) + sh2
        xs = xs + g2 * peer_ffn(h, peer_wq[l], peer_keys[l], peer_u[l], peer_v[l])

    new_a_k = jnp.stack(new_ak, axis=1)
    new_a_v = jnp.stack(new_av, axis=1)
    new_b_k = jnp.stack(new_bk, axis=1)
    new_b_v = jnp.stack(new_bv, axis=1)
    return (xp, xs, new_a_k, new_a_v, new_b_k, new_b_v)


_drawn_inputs = setup_inputs


def setup_inputs(seed=0):
    import zlib

    import numpy as np

    out = dict(_drawn_inputs(seed))
    spreads = {}
    factors = {'qn_a': 4.522,
     'kn_a': 2.785,
     'qn_b': 4.898,
     'lam_q1': 4.209,
     'lam_q2': 4.907,
     'lam_k2': 4.772,
     'subln_g': 3.103,
     'out_norm_a': 3.056,
     'out_norm_c': 3.379,
     'conv_b': 3.322,
     'cache_a_k': 8.0,
     'cache_a_v': 8.0}
    for name, (base, spread) in spreads.items():
        noise = np.random.default_rng([zlib.crc32(name.encode()), seed]).standard_normal(out[name].shape)
        drawn = base * np.exp(spread * noise) if base else spread * noise
        out[name] = __import__('jax').numpy.asarray(drawn.astype(out[name].dtype))
    for name, factor in factors.items():
        out[name] = (out[name] * factor).astype(out[name].dtype)
    return out
```

```python
from contextlib import ExitStack

import numpy as np

import concourse.bass as bass
from concourse import mybir

F32 = mybir.dt.float32
U32 = mybir.dt.uint32
ALU = mybir.AluOpType
ACT = mybir.ActivationFunctionType
AXX = mybir.AxisListType.X

P = 128
DM = 1024
KC = DM // P
DEPTH = 2
T = 3
COND = (1, 0, 0)
EPS = 1e-6
HD, DK = 64, 32
A_HEADS, A_KV, B_HEADS, CW = 6, 2, 6, 256
AW, BW = A_HEADS * HD, B_HEADS * HD
QA, KA, VA = 0, AW, AW + A_KV * HD
QB = VA + A_KV * HD
KB, VB = QB + BW, QB + 2 * BW
CI = VB + BW
CB, CC = CI + CW, CI + 2 * CW
DPROJ = CC + CW
GA, GB = (VA - QA) // HD, (VB - QB) // DK
N_KEYS = 128
P_HEADS, TOPK = 8, 16
N_EXPERTS = N_KEYS * N_KEYS
NH = T * P_HEADS
GRID_W, ROPE_BASE = 64, 10000.0
PAST = 128

NB = 512
ADA_CHUNKS = 6 * DM // NB
IN_CHUNKS = DPROJ // NB
OUT_CHUNKS = DM // NB
Q_CHUNKS = P_HEADS * 2 * P // NB
C_IN = ADA_CHUNKS
C_OUT = C_IN + IN_CHUNKS
C_KEYS = C_OUT + OUT_CHUNKS
C_Q = C_KEYS + 1
CHUNKS = C_Q + Q_CHUNKS
WRING = 3
URING, VRING, DRING = 16, 8, 4
UNITS = A_HEADS + 2 * B_HEADS
HEADS = A_HEADS + B_HEADS
SLOTS = ((0,), (1, 2, 3), (1, 2, 3))
GELU_A = 0.044715
GELU_B = float(np.sqrt(2.0 / np.pi))
NEG = -3.0e38

PARAMS = {}
_at = 0
for _name, _n in (("qn_a", HD), ("kn_a", HD), ("qn_b", DK), ("kn_b", DK), ("lam_q1", DK), ("lam_k1", DK),
                  ("lam_q2", DK), ("lam_k2", DK), ("subln_g", HD), ("out_norm_a", AW), ("out_norm_c", CW),
                  ("conv_w", 3 * CW), ("conv_b", CW), ("depth", 4)):
    PARAMS[_name] = (_at, _at + _n)
    _at += _n
N_PARAMS = _at

C_ID, C_ZERO, C_IOTA, C_EPS, C_SEL = 0, P, 2 * P, 2 * P + TOPK, 2 * P + TOPK + 1
N_CONST = C_SEL + 2 * P
D_DOWN, D_UP, D_EPREV, D_ENEXT, D_ROPE = 0, P, 2 * P, 3 * P, 4 * P
ROPE_W = 2 * HD + 2 * DK
N_DENSE = D_ROPE + 2 * ROPE_W


class Steps:

    def __init__(self, engine, sem, waited=None):
        self.engine, self.sem, self.base, self.n = engine, sem, 0, 0
        self.waited = waited

    def before_search(self, ins):
        self.after(ins)
        self.engine.sem_inc(self.waited, 1)

    def after(self, ins):
        self.n += 1
        ins.then_inc(self.sem, 1)
        self.engine.wait_ge(self.sem, self.base + self.n)

    def enter(self, i, per):
        self.saved = self.base, self.n
        self.base, self.n = self.base + self.n + i * per, 0

    def leave(self, trips, per):
        assert self.n == per, (self.n, per)
        self.base, self.n = self.saved[0], self.saved[1] + trips * per


def build(nc, x_prompt, x_sample, cache_a_k, cache_a_v, cache_b_k, cache_b_v, cond, ada_w, ada_b, norm_g,
          w_in, params, w_out, peer_wq, peer_keys, peer_u, peer_v, const, dense_const,
          y_prompt, y_sample, new_a_k, new_a_v, new_b_k, new_b_v, link_counts):
    with ExitStack() as ctx:
        def sb(name, shape, dt=F32):
            return ctx.enter_context(nc.sbuf_tensor(name, shape, dt))

        def psum(name):
            return ctx.enter_context(nc.psum_tensor(name, [P, 2 * NB], F32))

        def sem(name):
            return ctx.enter_context(nc.semaphore(name))

        x = sb("x", [P, T, DM])
        consts = sb("consts", [P, N_CONST])
        condT = sb("condT", [P, KC, 2])
        gate2_rows = sb("gate2_rows", [2, DM])
        ident = consts[:, C_ID:C_ID + P]
        zeros = consts[:, C_ZERO:C_ZERO + P]
        iota16 = consts[:, C_IOTA:C_IOTA + TOPK]
        eps = consts[:, C_EPS:C_EPS + 1]

        def select(c):
            return consts[0:2, C_SEL + c * P:C_SEL + (c + 1) * P]

        weights = sb("weights", [P, WRING, KC, NB])

        region = sb("region", [P, (URING + VRING) * DM])
        u_ring = region[:, 0:URING * DM].rearrange("p (s d) -> p s d", d=DM)
        v_ring = region[:, URING * DM:].rearrange("p (s d) -> p s d", d=DM)
        top = [0]

        def carve(n, of=region):
            a = top[0]
            top[0] += n
            assert top[0] <= of.shape[1]
            return of[:, a:a + n]

        mod_rows = carve(6 * DM)[0:2, :]
        norm_rows = carve(2 * DM)[0:2, :]
        proj_flat = carve(T * DPROJ)
        proj = proj_flat.rearrange("p (t n) -> p t n", t=T)
        hT = carve(KC * T * P).rearrange("p (k n) -> p k n", k=KC)
        par = carve(N_PARAMS)
        dense = carve(N_DENSE)
        qT = carve(6 * P).rearrange("p (c n) -> p c n", c=6)
        keysT = proj_flat[:, 0:2 * P_HEADS * P].rearrange("p (i n) -> p i n", n=P)
        pqT = proj_flat[:, 2 * P_HEADS * P:2 * P_HEADS * P + 4 * T * P].rearrange("p (r n) -> p r n", r=4)

        scores_flat = sb("scores", [P, NH * 2 * N_KEYS])
        peer_scores = scores_flat[:].rearrange("p (n m) -> p n m", m=2 * N_KEYS)
        top[0] = 0
        probs = carve(4 * 3 * P, scores_flat).rearrange("p (r n) -> p r n", r=4)
        probsT = carve(2 * 3 * P, scores_flat).rearrange("p (r n) -> p r n", r=2)
        scratch = carve(VB, scores_flat)
        merged = carve(DM, scores_flat)
        conv_u = carve(T * CW, scores_flat).rearrange("p (t n) -> p t n", t=T)

        h2 = sb("h2", [P, T, DM])
        h2_flat = h2[:].rearrange("p t d -> p (t d)")
        top[0] = 0
        kT_a = carve(4 * P, h2_flat).rearrange("p (j n) -> p j n", j=4)
        kT_b = carve(12 * P, h2_flat).rearrange("p (c j n) -> p c j n", c=3, j=4)
        past_va = carve(P, h2_flat)
        past_vb = carve(BW, h2_flat)
        past_ka = carve(P, h2_flat)
        past_kb = carve(BW, h2_flat)

        sumsq = sb("sumsq", [P, 4])
        rstd = sb("rstd", [P, 4])
        qk_ms = sb("qk_ms", [P, T, GA + GB])
        qk_root = sb("qk_root", [P, T, GA + GB])
        rowmax = sb("rowmax", [P, UNITS])
        negmax = sb("negmax", [P, UNITS])
        rowsum = sb("rowsum", [P, UNITS])
        rinv = sb("rinv", [P, UNITS])
        merge_ms = sb("merge_ms", [P, 8])
        merge_root = sb("merge_root", [P, 8])
        lam_work = sb("lam_work", [P, 8])
        layer_base = sb("layer_base", [P, 1])
        cond_work = sb("cond_work", [P, 2, KC, 2])
        st = sb("st", [P, 2 * N_KEYS])
        st_rest = sb("st_rest", [P, 2 * N_KEYS])
        cand = sb("cand", [P, TOPK, TOPK])
        half_top = sb("half_top", [P, 2, TOPK])
        half_idx = sb("half_idx", [P, 2, TOPK], U32)
        half_idx_f = sb("half_idx_f", [P, 2, TOPK])
        pair_top = sb("pair_top", [P, 2, TOPK])
        pair_pos = sb("pair_pos", [P, TOPK], U32)
        pair_ab = sb("pair_ab", [P, 2, TOPK], U32)
        pair_ab_f = sb("pair_ab_f", [P, 2, TOPK])
        pair_key = sb("pair_key", [P, 2, TOPK])
        idx_f = sb("idx_f", [P, TOPK])
        expert = sb("expert", [P, 2, TOPK], U32)
        gathered = sb("gathered", [P, 2, TOPK], U32)
        pair_neg = sb("pair_neg", [P, 2])
        gate = sb("gate", [P, 2, TOPK])
        gate_sum = sb("gate_sum", [P, 2])
        gate_inv = sb("gate_inv", [P, 1])
        dots = sb("dots", [P, 2, TOPK])
        poly = sb("poly", [P, 2, TOPK])
        gexp = sb("gexp", [P, TOPK])
        act_work = sb("act_work", [P, TOPK])
        coef = sb("coef", [P, 2, TOPK])
        diag = sb("diag", [P, DRING, P])

        ps_acc = psum("ps_acc")
        ps_mb = psum("ps_mb")
        ps_mm = psum("ps_mm")
        ps_tr = psum("ps_tr")

        def mm(i, n=NB):
            return ps_mm[:, (i % 2) * NB:(i % 2) * NB + n]

        def tr(i, n=NB):
            return ps_tr[:, (i % 2) * NB:(i % 2) * NB + n]

        const_loaded = sem("const_loaded")
        w_full = [sem(f"w_full{i}") for i in range(WRING)]
        ring_idle = sem("ring_idle")
        params_loaded = sem("params_loaded")
        layer_done = sem("layer_done")
        cond_ready = sem("cond_ready")
        cond_exp = sem("cond_exp")
        mod_mm = sem("mod_mm")
        mod_row = sem("mod_row")
        mod_ready = sem("mod_ready")
        rms_root = sem("rms_root")
        gain_bc = sem("gain_bc")
        shift_bc = sem("shift_bc")
        h_ready = sem("h_ready")
        h_mm = sem("h_mm")
        hT_ready = sem("hT_ready")
        proj_mm = sem("proj_mm")
        proj_ready = sem("proj_ready")
        qk_meansq = sem("qk_meansq")
        qk_rooted = sem("qk_rooted")
        kv_ready = sem("kv_ready")
        kv_stored = sem("kv_stored")
        qk_ready = sem("qk_ready")
        lam_sums = sem("lam_sums")
        lam_exps = sem("lam_exps")
        kT_mm = sem("kT_mm")
        kT_ready = sem("kT_ready")
        qT_mm = sem("qT_mm")
        qT_ready = sem("qT_ready")
        score_mm = sem("score_mm")
        negmax_ready = sem("negmax_ready")
        exp_ready = sem("exp_ready")
        mix_ready = sem("mix_ready")
        pT_mm = sem("pT_mm")
        pT_ready = sem("pT_ready")
        pv_done = sem("pv_done")
        conv_mm = sem("conv_mm")
        conv_read = sem("conv_read")
        merge_meansq = sem("merge_meansq")
        merge_rooted = sem("merge_rooted")
        merged_ready = sem("merged_ready")
        mergedT_mm = sem("mergedT_mm")
        mergedT_ready = sem("mergedT_ready")
        out_mm = sem("out_mm")
        out_copied = sem("out_copied")
        x_mixed = sem("x_mixed")
        keys_ready = sem("keys_ready")
        pq_mm = sem("pq_mm")
        pq_ready = sem("pq_ready")
        ps_done = sem("ps_done")
        ps_ready = sem("ps_ready")
        expert_ready = sem("expert_ready")
        expert_taken = sem("expert_taken")
        gate_max = sem("gate_max")
        gate_exp = sem("gate_exp")
        u_full = [sem(f"u_full{k}") for k in range(URING)]
        u_used = sem("u_used")
        v_full = [sem(f"v_full{k}") for k in range(VRING)]
        v_used = sem("v_used")
        poly_ready = sem("poly_ready")
        gexp_ready = sem("gexp_ready")
        coef_ready = sem("coef_ready")
        diag_ready = sem("diag_ready")
        acc_done = sem("acc_done")
        acc_copied = sem("acc_copied")
        x_fed = sem("x_fed")
        y_stored = sem("y_stored")
        gather_may = sem("gather_may")
        search_may = sem("search_may")
        dve_step = sem("dve_step")
        act_step = sem("act_step")

        block = ctx.enter_context(nc.Block())

        def pcol(name):
            a, b = PARAMS[name]
            return par[:, a:b]

        def units(head):
            return (head,) if head < A_HEADS else (2 * head - A_HEADS, 2 * head - A_HEADS + 1)

        @block.sync
        def _(sp):
            sp.dma_start(consts[:], const).then_inc(const_loaded, 16)
            sp.dma_start(x[:, 0, :], x_prompt[0]).then_inc(const_loaded, 16)
            sp.dma_start(x[:, 1:3, :], x_sample[0].rearrange("(t p) d -> p t d", p=P)).then_inc(const_loaded, 16)
            with nc.allow_non_contiguous_dma("the conditioning vectors, 8 KB"):
                for c in range(2):
                    sp.dma_start(cond_work[:, 0, :, c], cond[c].rearrange("(k p) -> p k", p=P)).then_inc(const_loaded, 16)

            def used(l, c):
                if c < C_IN:
                    return mod_mm, l * ADA_CHUNKS + c + 1
                if c < C_OUT:
                    return proj_mm, l * IN_CHUNKS * T + (c - C_IN + 1) * T
                if c < C_KEYS:
                    return out_mm, l * OUT_CHUNKS * T + (c - C_OUT + 1) * T
                if c == C_KEYS:
                    return keys_ready, l + 1
                return pq_mm, l * 16 + (c - C_Q + 1) * 4

            def chunk(l, c, src):
                sp.wait_ge(*(used(l, c - WRING) if c >= WRING else (ring_idle, l + 1)))
                dst = weights[:, c % WRING, :, :]
                if c == C_KEYS:
                    dst = dst.rearrange("p k n -> p (k n)")[:, 0:2 * P_HEADS * P]
                sp.dma_start(dst, src).then_inc(w_full[c % WRING], 16)

            def columns(w, n):
                return w.rearrange("o (k p) n -> p (o k) n", p=P)[:, :, n * NB:(n + 1) * NB]

            with sp.Fori(0, DEPTH) as l:
                layer = bass.ds(l, 1)
                for n in range(WRING):
                    chunk(l, n, columns(ada_w[layer], n))
                sp.wait_ge(layer_done, l + 1)
                sp.dma_start(par, params[layer, :].partition_broadcast(P).rearrange("p o n -> p (o n)")).then_inc(params_loaded, 16)
                sp.dma_start(dense, dense_const).then_inc(params_loaded, 16)
                sp.dma_start(mod_rows, ada_b[layer, :].partition_broadcast(2).rearrange("p o n -> p (o n)")).then_inc(params_loaded, 16)
                sp.dma_start(norm_rows, norm_g[layer, :].partition_broadcast(2).rearrange("p o n -> p (o n)")).then_inc(params_loaded, 16)
                sp.dma_start(past_ka, cache_a_k[0, layer].rearrange("o s k d -> s (o k d)")).then_inc(params_loaded, 16)
                sp.dma_start(past_va, cache_a_v[0, layer].rearrange("o s k d -> s (o k d)")).then_inc(params_loaded, 16)
                sp.dma_start(past_kb, cache_b_k[0, layer].rearrange("o s h j d -> s (o h j d)")).then_inc(params_loaded, 16)
                sp.dma_start(past_vb, cache_b_v[0, layer].rearrange("o s h d -> s (o h d)")).then_inc(params_loaded, 16)
                for n in range(WRING, ADA_CHUNKS):
                    chunk(l, n, columns(ada_w[layer], n))
                for n in range(IN_CHUNKS):
                    chunk(l, C_IN + n, columns(w_in[layer], n))
                for n in range(OUT_CHUNKS):
                    chunk(l, C_OUT + n, columns(w_out[layer], n))
                chunk(l, C_KEYS, peer_keys[layer].rearrange("o d n -> d (o n)"))
                sp.wait_ge(kv_ready, l + 1)
                sp.dma_start(new_a_k[0, layer].rearrange("o s k d -> s (o k d)"), proj[:, 0, KA:VA]).then_inc(kv_stored, 16)
                sp.dma_start(new_a_v[0, layer].rearrange("o s k d -> s (o k d)"), proj[:, 0, VA:QB]).then_inc(kv_stored, 16)
                sp.dma_start(new_b_k[0, layer].rearrange("o s h j d -> s (o h j d)"), proj[:, 0, KB:VB]).then_inc(kv_stored, 16)
                sp.dma_start(new_b_v[0, layer].rearrange("o s h d -> s (o h d)"), proj[:, 0, VB:CI]).then_inc(kv_stored, 16)
                for n in range(Q_CHUNKS):
                    chunk(l, C_Q + n, columns(peer_wq[layer], n))
            sp.wait_ge(layer_done, DEPTH + 1)
            sp.dma_start(y_prompt[0], x[:, 0, :]).then_inc(y_stored, 16)
            sp.dma_start(y_sample[0].rearrange("(t p) d -> p t d", p=P), x[:, 1:3, :]).then_inc(y_stored, 16)
            sp.wait_ge(y_stored, 32)
            sp.wait_ge(kv_stored, DEPTH * 64)

        @block.gpsimd
        def _(pool):
            pool.sem_inc(expert_taken, 2)
            with pool.Fori(0, DEPTH) as l:
                with pool.Fori(0, NH // 2) as i:
                    for p in range(2):
                        n = l * NH + i * 2 + p
                        pool.wait_ge(expert_ready, n + 1)
                        pool.sem_inc(gather_may, 1)
                        pool.tensor_copy(gathered[:, p, :], expert[:, p, :]).then_inc(expert_taken, 1)
                        pool.wait_ge(expert_taken, n + 3)
                        for k in range(TOPK):
                            pool.wait_ge(u_used, n * TOPK + k + 1)
                            pool.sem_inc(gather_may, 1)
                            pool.indirect_dma_start(
                                u_ring[:, k, :], None, peer_u,
                                bass.IndirectOffsetOnAxis(ap=gathered[:, p, k:k + 1], axis=0)).then_inc(u_full[k], 16)
                        for k in range(TOPK):
                            pool.wait_ge(v_used, n * TOPK + k + 1)
                            pool.sem_inc(gather_may, 1)
                            pool.indirect_dma_start(
                                v_ring[:, k % VRING, :], None, peer_v,
                                bass.IndirectOffsetOnAxis(ap=gathered[:, p, k:k + 1], axis=0)).then_inc(v_full[k % VRING], 16)

        @block.tensor
        def _(pe):
            pe.sem_inc(ring_idle, 1)
            pe.sem_inc(v_used, VRING)
            pe.wait_ge(const_loaded, 5 * 16)
            pe.wait_ge(cond_ready, 1)

            with pe.Fori(0, DEPTH) as l:
                def arrived(c):
                    pe.wait_ge(w_full[c % WRING], (l * (CHUNKS // WRING) + c // WRING + 1) * 16)
                    return weights[:, c % WRING]

                def broadcast(out, rows, c):
                    for n in range(2):
                        last = pe.matmul(out[:, n * NB:(n + 1) * NB], select(c), rows[0:2, n * NB:(n + 1) * NB],
                                         start=True, stop=True)
                    return last

                pe.wait_ge(layer_done, l + 1)
                for n in range(ADA_CHUNKS):
                    w = arrived(n)
                    if n >= 2:
                        pe.wait_ge(mod_row, l * ADA_CHUNKS + n - 1)
                    for k in range(KC):
                        last = pe.matmul(mm(n)[0:2, :], condT[:, k, :], w[:, k, :], start=(k == 0), stop=(k == KC - 1))
                    last.then_inc(mod_mm, 1)
                pe.wait_ge(mod_ready, l + 1)

                def norm(stage):
                    gain = mod_rows[:, (3 * stage + 1) * DM:(3 * stage + 2) * DM]
                    shift = mod_rows[:, 3 * stage * DM:(3 * stage + 1) * DM]
                    for t in range(T):
                        m = l * 2 * T + stage * T + t
                        broadcast(ps_mb[:], gain, COND[t]).then_inc(gain_bc, 1)
                        broadcast(ps_mm[:], shift, COND[t]).then_inc(shift_bc, 1)
                        pe.wait_ge(h_ready, m + 1)
                        if t:
                            pe.wait_ge(hT_ready, m)
                        src = merged if stage == 0 else h2[:, t, :]
                        for k in range(KC):
                            last = pe.transpose(ps_tr[:, k * P:(k + 1) * P], src[:, k * P:(k + 1) * P], ident)
                        last.then_inc(h_mm, 1)
                    pe.wait_ge(hT_ready, l * 2 * T + (stage + 1) * T)

                norm(0)

                for n in range(IN_CHUNKS):
                    w = arrived(C_IN + n)
                    for t in range(T):
                        i = n * T + t
                        if i >= 2:
                            pe.wait_ge(proj_ready, l * IN_CHUNKS * T + i - 1)
                        for k in range(KC):
                            last = pe.matmul(mm(i), hT[:, k, t * P:(t + 1) * P], w[:, k, :],
                                             start=(k == 0), stop=(k == KC - 1))
                        last.then_inc(proj_mm, 1)

                pe.wait_ge(qk_ready, l + 1)
                pe.wait_ge(params_loaded, (l + 1) * 8 * 16)
                for j in range(4):
                    if j >= 2:
                        pe.wait_ge(kT_ready, l * 4 + j - 1)
                    ka = proj[:, j, KA:VA] if j < 3 else past_ka
                    kb = proj[:, j, KB:VB] if j < 3 else past_kb
                    pe.transpose(tr(j)[:, 0:P], ka, ident)
                    for c in range(3):
                        last = pe.transpose(tr(j)[:, (c + 1) * P:(c + 2) * P], kb[:, c * P:(c + 1) * P], ident)
                    last.then_inc(kT_mm, 1)
                pe.wait_ge(kT_ready, l * 4 + 4)

                for t in range(T):
                    slots = SLOTS[t]
                    nk = len(slots)
                    if t:
                        pe.wait_ge(conv_read, l * T + t)
                    pe.matmul(ps_mb[:, 0:CW], dense[:, D_DOWN:D_DOWN + P], conv_u[:, t, :], start=True, stop=(t != 2))
                    if t == 2:
                        pe.matmul(ps_mb[:, 0:CW], dense[:, D_EPREV:D_EPREV + P], conv_u[:, 1, :], start=False, stop=True)
                    last = pe.matmul(ps_mb[:, NB:NB + CW], dense[:, D_UP:D_UP + P], conv_u[:, t, :], start=True, stop=(t != 1))
                    if t == 1:
                        last = pe.matmul(ps_mb[:, NB:NB + CW], dense[:, D_ENEXT:D_ENEXT + P], conv_u[:, 2, :],
                                         start=False, stop=True)
                    last.then_inc(conv_mm, 1)
                    if t:
                        pe.wait_ge(mergedT_ready, l * T + t)
                    for r in range(3):
                        pe.transpose(ps_tr[:, r * P:(r + 1) * P], proj[:, t, QA + r * P:QA + (r + 1) * P], ident)
                    for c in range(3):
                        last = pe.transpose(ps_tr[:, (3 + c) * P:(4 + c) * P], proj[:, t, QB + c * P:QB + (c + 1) * P], ident)
                    last.then_inc(qT_mm, 1)
                    pe.wait_ge(qT_ready, l * T + t + 1)

                    def scores(head):
                        for u in units(head):
                            g = t * UNITS + u
                            if g >= 2:
                                pe.wait_ge(exp_ready, l * T * UNITS + g - 1)
                            out = mm(g, nk * P)
                            if u < A_HEADS:
                                lo = HD * (u // 3)
                                q = qT[lo:lo + HD, u % 3, :]
                                k = kT_a[lo:lo + HD, slots[0]:slots[0] + nk, :]
                            else:
                                m = u - A_HEADS
                                lo = DK * (m % 4)
                                q = qT[lo:lo + DK, 3 + m // 4, :]
                                k = kT_b[lo:lo + DK, m // 4, slots[0]:slots[0] + nk, :]
                            pe.matmul(out, q, k.rearrange("p j n -> p (j n)"), start=True, stop=True,
                                      tile_position=(lo, 0)).then_inc(score_mm, 1)

                    def transpose_probs(head):
                        u = units(head)[0]
                        if head < A_HEADS:
                            pe.wait_ge(exp_ready, l * T * UNITS + t * UNITS + u + 1)
                        else:
                            pe.wait_ge(mix_ready, l * T * B_HEADS + t * B_HEADS + head - A_HEADS + 1)
                        if head >= 2:
                            pe.wait_ge(pT_ready, l * T * HEADS + t * HEADS + head - 1)
                        for j in range(nk):
                            last = pe.transpose(tr(head)[:, j * P:(j + 1) * P], probs[:, (t * UNITS + u) % 4, j * P:(j + 1) * P], ident)
                        last.then_inc(pT_mm, 1)

                    def weigh_values(head):
                        pe.wait_ge(pT_ready, l * T * HEADS + t * HEADS + head + 1)
                        for j, s in enumerate(slots):
                            if head < A_HEADS:
                                col, kv = head * HD, (head // 3) * HD
                                v = proj[:, s, VA + kv:VA + kv + HD] if s < 3 else past_va[:, kv:kv + HD]
                            else:
                                hb = (head - A_HEADS) * HD
                                col = NB + hb
                                v = proj[:, s, VB + hb:VB + hb + HD] if s < 3 else past_vb[:, hb:hb + HD]
                            last = pe.matmul(ps_acc[:, col:col + HD], probsT[:, head % 2, j * P:(j + 1) * P], v,
                                             start=(j == 0), stop=(j == nk - 1))
                        last.then_inc(pv_done, 1)

                    scores(0)
                    for head in range(HEADS):
                        if head + 1 < HEADS:
                            scores(head + 1)
                        transpose_probs(head)
                        if head:
                            weigh_values(head - 1)
                    weigh_values(HEADS - 1)

                    pe.wait_ge(merged_ready, l * T + t + 1)
                    pe.wait_ge(pT_ready, l * T * HEADS + (t + 1) * HEADS)
                    for k in range(KC):
                        last = pe.transpose(ps_tr[:, k * P:(k + 1) * P], merged[:, k * P:(k + 1) * P], ident)
                    last.then_inc(mergedT_mm, 1)

                pe.wait_ge(mergedT_ready, (l + 1) * T)
                for n in range(OUT_CHUNKS):
                    w = arrived(C_OUT + n)
                    for t in range(T):
                        i = n * T + t
                        if i >= 2:
                            pe.wait_ge(out_copied, l * OUT_CHUNKS * T + i - 1)
                            pe.wait_ge(x_mixed, l * OUT_CHUNKS * T + i - 1)
                        for k in range(KC):
                            pe.matmul(mm(i), hT[:, k, t * P:(t + 1) * P], w[:, k, :], start=(k == 0), stop=(k == KC - 1))
                        pe.matmul(ps_mb[:, (i % 2) * NB:(i % 2 + 1) * NB], select(COND[t]),
                                  mod_rows[:, 2 * DM + n * NB:2 * DM + (n + 1) * NB],
                                  start=True, stop=True).then_inc(out_mm, 1)

                pe.wait_ge(x_mixed, (l + 1) * OUT_CHUNKS * T)
                norm(1)

                pe.wait_ge(keys_ready, l + 1)

                def half_scores(i):
                    pe.wait_ge(pq_ready, l * 16 + i + 1)
                    if i >= 2:
                        pe.wait_ge(ps_ready, l * 16 + i - 1)
                    for t in range(T):
                        last = pe.matmul(tr(i)[:, t * P:(t + 1) * P], pqT[:, i % 4, t * P:(t + 1) * P], keysT[:, i, :],
                                         start=True, stop=True)
                    last.then_inc(ps_done, 1)

                for n in range(Q_CHUNKS):
                    w = arrived(C_Q + n)
                    for j in range(4):
                        i = 4 * n + j
                        if i >= 2:
                            pe.wait_ge(pq_ready, l * 16 + i - 1)
                        for k in range(KC):
                            last = pe.matmul(mm(i, T * P), w[:, k, j * P:(j + 1) * P], hT[:, k, :],
                                             start=(k == 0), stop=(k == KC - 1))
                        last.then_inc(pq_mm, 1)
                        if i:
                            half_scores(i - 1)
                half_scores(15)
                pe.sem_inc(ring_idle, 1)

                for t in range(T):
                    if t:
                        pe.wait_ge(acc_copied, l * T + t)
                    for n in range(2):
                        pe.matmul(ps_acc[:, n * NB:(n + 1) * NB], zeros, consts[:, 0:NB], start=True, stop=False)
                    with pe.Fori(0, P_HEADS // 2) as i:
                        for p in range(2):
                            m = l * NH + (t * P_HEADS + p) + i * 2
                            for k in range(TOPK):
                                pe.wait_ge(diag_ready, m * TOPK + k + 1)
                                pe.wait_ge(v_full[k % VRING], (m * 2 + k // VRING + 1) * 16)
                                for n in range(2):
                                    last = pe.matmul(ps_acc[:, n * NB:(n + 1) * NB], diag[:, k % DRING, :],
                                                     v_ring[:, k % VRING, n * NB:(n + 1) * NB], start=False, stop=False)
                                last.then_inc(v_used, 1)
                    for n in range(2):
                        pe.matmul(ps_acc[:, n * NB:(n + 1) * NB], zeros, consts[:, 0:NB], start=False, stop=True)
                    if t:
                        pe.wait_ge(x_fed, l * T + t)
                    broadcast(ps_mb[:], gate2_rows, COND[t]).then_inc(acc_done, 1)

        @block.scalar
        def _(act):
            step = Steps(act, act_step)
            act.wait_ge(const_loaded, 5 * 16)
            act.activation(cond_work[:, 1], cond_work[:, 0], ACT.Exp, scale=-1.0).then_inc(cond_exp, 1)
            with act.Fori(0, DEPTH) as l:
                act.wait_ge(layer_done, l + 1)

                def norm(stage):
                    for t in range(T):
                        step.after(act.activation(scratch[:, 0:DM], x[:, t, :], ACT.Square, accum_out=sumsq[:, t:t + 1]))
                    act.activation(rstd[:, 0:T], sumsq[:, 0:T], ACT.Sqrt, bias=eps, scale=1.0 / DM).then_inc(rms_root, 1)
                    for t in range(T):
                        act.wait_ge(h_mm, l * 2 * T + stage * T + t + 1)
                        act.activation(hT[:, :, t * P:(t + 1) * P], ps_tr[:].rearrange("p (k n) -> p k n", k=KC),
                                       ACT.Copy).then_inc(hT_ready, 1)

                step.enter(l, 2 * T)
                norm(0)
                for i in range(IN_CHUNKS * T):
                    act.wait_ge(proj_mm, l * IN_CHUNKS * T + i + 1)
                    n, t = i // T, i % T
                    if n == 0:
                        act.activation(proj[:, t, QA:KA].rearrange("p (r g d) -> p r g d", g=2, r=3),
                                       mm(i)[:, QA:KA].rearrange("p (g r d) -> p r g d", g=2, r=3), ACT.Copy)
                        act.activation(proj[:, t, KA:NB], mm(i)[:, KA:NB], ACT.Copy).then_inc(proj_ready, 1)
                    else:
                        act.activation(proj[:, t, n * NB:(n + 1) * NB], mm(i), ACT.Copy).then_inc(proj_ready, 1)
                act.wait_ge(qk_meansq, l + 1)
                act.activation(qk_root[:], qk_ms[:], ACT.Sqrt).then_inc(qk_rooted, 1)
                act.wait_ge(lam_sums, l + 1)
                act.activation(lam_work[:, 2:4], lam_work[:, 0:2], ACT.Exp).then_inc(lam_exps, 1)
                for j in range(4):
                    act.wait_ge(kT_mm, l * 4 + j + 1)
                    act.activation(kT_a[:, j, :], tr(j)[:, 0:P], ACT.Copy)
                    act.activation(kT_b[:, :, j, :], tr(j)[:, P:4 * P].rearrange("p (c n) -> p c n", c=3),
                                   ACT.Copy).then_inc(kT_ready, 1)
                for t in range(T):
                    nk = len(SLOTS[t])
                    act.wait_ge(qT_mm, l * T + t + 1)
                    act.activation(qT, ps_tr[:, 0:6 * P].rearrange("p (c n) -> p c n", c=6), ACT.Copy).then_inc(qT_ready, 1)

                    def exps(head):
                        for u in units(head):
                            g = t * UNITS + u
                            act.wait_ge(negmax_ready, l * T * UNITS + g + 1)
                            if head >= 2:
                                act.wait_ge(pT_mm, l * T * HEADS + t * HEADS + head - 1)
                            act.activation(probs[:, g % 4, 0:nk * P], mm(g, nk * P), ACT.Exp, bias=negmax[:, u:u + 1],
                                           scale=float(HD if u < A_HEADS else DK) ** -0.5,
                                           accum_out=rowsum[:, u:u + 1]).then_inc(exp_ready, 1)

                    exps(0)
                    for head in range(HEADS):
                        if head + 1 < HEADS:
                            exps(head + 1)
                        act.wait_ge(pT_mm, l * T * HEADS + t * HEADS + head + 1)
                        if head >= 2:
                            act.wait_ge(pv_done, l * T * HEADS + t * HEADS + head - 1)
                        act.activation(probsT[:, head % 2, 0:nk * P], tr(head, nk * P), ACT.Copy).then_inc(pT_ready, 1)
                    act.wait_ge(merge_meansq, l * T + t + 1)
                    act.activation(merge_root[:], merge_ms[:], ACT.Sqrt).then_inc(merge_rooted, 1)
                    act.wait_ge(mergedT_mm, l * T + t + 1)
                    act.activation(hT[:, :, t * P:(t + 1) * P], ps_tr[:].rearrange("p (k n) -> p k n", k=KC),
                                   ACT.Copy).then_inc(mergedT_ready, 1)
                for i in range(OUT_CHUNKS * T):
                    act.wait_ge(out_mm, l * OUT_CHUNKS * T + i + 1)
                    if i >= 2:
                        act.wait_ge(x_mixed, l * OUT_CHUNKS * T + i - 1)
                    act.activation(merged[:, (i % 2) * NB:(i % 2 + 1) * NB], mm(i), ACT.Copy).then_inc(out_copied, 1)
                act.wait_ge(x_mixed, (l + 1) * OUT_CHUNKS * T)
                norm(1)
                step.leave(DEPTH, 2 * T)
                act.wait_ge(kv_stored, (l + 1) * 64)
                act.wait_ge(w_full[C_KEYS % WRING], (l * (CHUNKS // WRING) + C_KEYS // WRING + 1) * 16)
                act.activation(keysT.rearrange("p i n -> p (i n)"),
                               weights[:, C_KEYS % WRING].rearrange("p k n -> p (k n)")[:, 0:2 * P_HEADS * P],
                               ACT.Copy).then_inc(keys_ready, 1)
                for i in range(16):
                    act.wait_ge(pq_mm, l * 16 + i + 1)
                    if i >= 4:
                        act.wait_ge(ps_done, l * 16 + i - 3)
                    act.activation(pqT[:, i % 4, :], mm(i, T * P), ACT.Copy).then_inc(pq_ready, 1)

                def gate_exps(m, p):
                    act.wait_ge(gate_max, m + 1)
                    act.activation(gate[:, p, :], pair_top[:, p, :], ACT.Exp, bias=pair_neg[:, p:p + 1],
                                   accum_out=gate_sum[:, p:p + 1]).then_inc(gate_exp, 1)

                def head_work(m, p):
                    act.wait_ge(poly_ready, m + 1)
                    act.activation(gexp[:], poly[:, p, :], ACT.Exp, scale=-2.0 * GELU_B).then_inc(gexp_ready, 1)
                    act.wait_ge(coef_ready, m + 1)
                    for k in range(TOPK):
                        act.wait_ge(v_used, m * TOPK + k + 1 + VRING - DRING)
                        act.activation(diag[:, k % DRING, :], ident, ACT.Copy, scale=coef[:, p, k:k + 1]).then_inc(diag_ready, 1)

                gate_exps(l * NH, 0)
                for t in range(T):
                    def pair(i, last=False):
                        m = l * NH + t * P_HEADS + i * 2
                        gate_exps(m + 1, 1)
                        head_work(m, 0)
                        if not last:
                            gate_exps(m + 2, 0)
                        head_work(m + 1, 1)
                    with act.Fori(0, P_HEADS // 2 - (t == T - 1)) as i:
                        pair(i)
                    if t == T - 1:
                        pair(P_HEADS // 2 - 1, last=True)
                    act.wait_ge(acc_done, l * T + t + 1)
                    act.activation(h2[:, t, :], ps_acc[:], ACT.Copy).then_inc(acc_copied, 1)

        @block.vector
        def _(dve):
            step = Steps(dve, dve_step, search_may)
            dve.sem_inc(layer_done, 1)
            dve.sem_inc(u_used, URING)
            dve.wait_ge(cond_exp, 1)
            step.after(dve.tensor_scalar(cond_work[:, 1], cond_work[:, 1], 1.0, None, ALU.add))
            step.after(dve.reciprocal(cond_work[:, 1], cond_work[:, 1]))
            dve.tensor_tensor(condT[:], cond_work[:, 0], cond_work[:, 1], ALU.mult).then_inc(cond_ready, 1)

            with dve.Fori(0, DEPTH) as l:
                step.enter(l, link_counts["layer"])
                dve.wait_ge(params_loaded, (l + 1) * 8 * 16)
                dve.tensor_copy(layer_base[:], pcol("depth")[:, 2:3])
                dve.tensor_tensor_reduce(st[:, 0:DK], pcol("lam_q1"), pcol("lam_k1"), 1.0, 0.0, ALU.mult, ALU.add,
                                         lam_work[:, 0:1])
                dve.tensor_tensor_reduce(st[:, DK:2 * DK], pcol("lam_q2"), pcol("lam_k2"), 1.0, 0.0, ALU.mult, ALU.add,
                                         lam_work[:, 1:2]).then_inc(lam_sums, 1)
                for n in range(ADA_CHUNKS):
                    dve.wait_ge(mod_mm, l * ADA_CHUNKS + n + 1)
                    row = mod_rows[:, n * NB:(n + 1) * NB]
                    dve.tensor_tensor(row, mm(n)[0:2, :], row, ALU.add).then_inc(mod_row, 1)
                dve.wait_ge(mod_row, (l + 1) * ADA_CHUNKS)
                for s in range(2):
                    row = mod_rows[:, (3 * s + 1) * DM:(3 * s + 2) * DM]
                    dve.scalar_tensor_tensor(out=row, in0=row, scalar=1.0, in1=norm_rows[:, s * DM:(s + 1) * DM],
                                             op0=ALU.add, op1=ALU.mult)
                dve.tensor_copy(gate2_rows[:], mod_rows[:, 5 * DM:6 * DM]).then_inc(mod_ready, 1)

                def norm(stage):
                    dve.wait_ge(rms_root, l * 2 + stage + 1)
                    step.after(dve.reciprocal(rstd[:, 0:T], rstd[:, 0:T]))
                    for t in range(T):
                        m = l * 2 * T + stage * T + t
                        h = merged if stage == 0 else h2[:, t, :]
                        dve.wait_ge(gain_bc, m + 1)
                        if stage == 0 and t:
                            dve.wait_ge(h_mm, m)
                        step.after(dve.scalar_tensor_tensor(out=h, in0=x[:, t, :], scalar=rstd[:, t:t + 1], in1=ps_mb[:],
                                                            op0=ALU.mult, op1=ALU.mult))
                        dve.wait_ge(shift_bc, m + 1)
                        dve.tensor_tensor(h, h, ps_mm[:], ALU.add).then_inc(h_ready, 1)

                norm(0)

                dve.wait_ge(proj_ready, (l + 1) * IN_CHUNKS * T)
                for t in range(T):
                    step.after(dve.tensor_tensor(scratch, proj[:, t, 0:VB], proj[:, t, 0:VB], ALU.mult))
                    dve.tensor_reduce(qk_ms[:, t, 0:GA], scratch[:, 0:VA].rearrange("p (g d) -> p g d", d=HD), AXX, ALU.add)
                    step.after(dve.tensor_reduce(qk_ms[:, t, GA:], scratch[:, QB:VB].rearrange("p (g d) -> p g d", d=DK),
                                                 AXX, ALU.add))
                dve.tensor_scalar(qk_ms[:, :, 0:GA], qk_ms[:, :, 0:GA], 1.0 / HD, EPS, ALU.mult, ALU.add)
                dve.tensor_scalar(qk_ms[:, :, GA:], qk_ms[:, :, GA:], 1.0 / DK, EPS, ALU.mult, ALU.add).then_inc(qk_meansq, 1)
                dve.wait_ge(qk_rooted, l + 1)
                step.after(dve.reciprocal(qk_root[:], qk_root[:]))
                for t in range(T):
                    va = proj[:, t, 0:VA].rearrange("p (g d) -> p g d", d=HD)
                    vb = proj[:, t, QB:VB].rearrange("p (g d) -> p g d", d=DK)

                    def rowwise(v, gain):
                        return gain.unsqueeze(1).broadcast_to(v.shape)

                    dve.tensor_tensor(va, va, qk_root[:, t, 0:GA].unsqueeze(2).broadcast_to(va.shape), ALU.mult)
                    step.after(dve.tensor_tensor(vb, vb, qk_root[:, t, GA:].unsqueeze(2).broadcast_to(vb.shape), ALU.mult))
                    for v, gain in ((va[:, 0:A_HEADS], "qn_a"), (va[:, A_HEADS:], "kn_a"),
                                    (vb[:, 0:2 * B_HEADS], "qn_b"), (vb[:, 2 * B_HEADS:], "kn_b")):
                        last = dve.tensor_tensor(v, v, rowwise(v, pcol(gain)), ALU.mult)
                    if t == 0:
                        last.then_inc(kv_ready, 1)
                        continue
                    step.after(last)
                    table = dense[:, D_ROPE + (t - 1) * ROPE_W:D_ROPE + t * ROPE_W]
                    for v, cos, sin, d in ((va, table[:, 0:HD], table[:, HD:2 * HD], HD),
                                           (vb, table[:, 2 * HD:2 * HD + DK], table[:, 2 * HD + DK:], DK)):
                        g, j = v.shape[1], d // 4
                        work = scratch[:, 0:g * d].rearrange("p (g d) -> p g d", d=d)
                        for axis in range(2):
                            for half in range(2):
                                at, other = (2 * axis + half) * j, (2 * axis + 1 - half) * j
                                last = dve.tensor_tensor(work[:, :, at:at + j], v[:, :, other:other + j],
                                                         rowwise(v[:, :, at:at + j], sin[:, at:at + j]), ALU.mult)
                        step.after(last)
                        step.after(dve.tensor_tensor(v, v, rowwise(v, cos), ALU.mult))
                        step.after(dve.tensor_tensor(v, v, work, ALU.add))
                dve.tensor_tensor(conv_u, proj[:, :, CC:], proj[:, :, CI:CB], ALU.mult).then_inc(qk_ready, 1)

                dve.wait_ge(lam_exps, l + 1)
                step.after(dve.tensor_tensor(lam_work[:, 4:5], lam_work[:, 3:4], lam_work[:, 2:3], ALU.subtract))
                neg_lam = lam_work[:, 5:6]
                step.after(dve.tensor_tensor(neg_lam, lam_work[:, 4:5], pcol("depth")[:, 0:1], ALU.subtract))

                for t in range(T):
                    nk = len(SLOTS[t])

                    def maxima(head):
                        for u in units(head):
                            g = t * UNITS + u
                            dve.wait_ge(score_mm, l * T * UNITS + g + 1)
                            step.after(dve.tensor_reduce(rowmax[:, u:u + 1], mm(g, nk * P), AXX, ALU.max))
                            dve.tensor_scalar(negmax[:, u:u + 1], rowmax[:, u:u + 1],
                                              -float(HD if u < A_HEADS else DK) ** -0.5, None,
                                              ALU.mult).then_inc(negmax_ready, 1)

                    def mix(head):
                        u = units(head)[0]
                        g = t * UNITS + u
                        dve.wait_ge(exp_ready, l * T * UNITS + g + 2)
                        step.after(dve.reciprocal(rinv[:, u:u + 2], rowsum[:, u:u + 2]))
                        dve.tensor_tensor(rinv[:, u + 1:u + 2], rinv[:, u + 1:u + 2], neg_lam, ALU.mult)
                        first = probs[:, g % 4, 0:nk * P]
                        step.after(dve.tensor_scalar(first, first, rinv[:, u:u + 1], None, ALU.mult))
                        dve.scalar_tensor_tensor(out=first, in0=probs[:, (g + 1) % 4, 0:nk * P], scalar=rinv[:, u + 1:u + 2],
                                                 in1=first, op0=ALU.mult, op1=ALU.add).then_inc(mix_ready, 1)

                    maxima(0)
                    for head in range(HEADS):
                        if head + 1 < HEADS:
                            maxima(head + 1)
                        if head >= A_HEADS:
                            mix(head)

                    if t:
                        dve.wait_ge(mergedT_mm, l * T + t)
                    yc = merged[:, AW + BW:]
                    tap = pcol("conv_w").rearrange("p (i n) -> p i n", i=3)
                    side = scratch[:, 0:CW]
                    dve.wait_ge(conv_mm, l * T + t + 1)
                    dve.tensor_tensor(yc, ps_mb[:, 0:CW], tap[:, 0], ALU.mult)
                    step.after(dve.tensor_tensor(side, conv_u[:, t, :], tap[:, 1], ALU.mult))
                    step.after(dve.tensor_tensor(yc, yc, side, ALU.add))
                    last = dve.tensor_tensor(side, ps_mb[:, NB:NB + CW], tap[:, 2], ALU.mult)
                    last.then_inc(conv_read, 1)
                    dve.wait_ge(conv_read, l * T + t + 1)
                    step.after(dve.tensor_tensor(yc, yc, side, ALU.add))
                    step.after(dve.tensor_tensor(yc, yc, pcol("conv_b"), ALU.add))
                    step.after(dve.tensor_tensor(yc, yc, proj[:, t, CB:CC], ALU.mult))

                    dve.wait_ge(exp_ready, l * T * UNITS + (t + 1) * UNITS)
                    step.after(dve.reciprocal(rinv[:, 0:A_HEADS], rowsum[:, 0:A_HEADS]))
                    dve.wait_ge(pv_done, l * T * HEADS + (t + 1) * HEADS)
                    ya = merged[:, 0:AW]
                    ya_heads = ya.rearrange("p (h d) -> p h d", d=HD)
                    yb = merged[:, AW:AW + BW]
                    yb_heads = yb.rearrange("p (h d) -> p h d", d=HD)
                    dve.tensor_tensor(ya_heads, ps_acc[:, 0:AW].rearrange("p (h d) -> p h d", d=HD),
                                      rinv[:, 0:A_HEADS].unsqueeze(2).broadcast_to(ya_heads.shape), ALU.mult)
                    step.after(dve.tensor_copy(yb, ps_acc[:, NB:NB + BW]))
                    dve.tensor_tensor_reduce(scratch[:, 0:AW], ya, ya, 1.0, 0.0, ALU.mult, ALU.add, merge_ms[:, 0:1])
                    dve.tensor_tensor_reduce(scratch[:, AW:AW + CW], yc, yc, 1.0, 0.0, ALU.mult, ALU.add, merge_ms[:, 1:2])
                    squares = scratch[:, AW + CW:AW + CW + BW]
                    step.after(dve.tensor_tensor(squares, yb, yb, ALU.mult))
                    step.after(dve.tensor_reduce(merge_ms[:, 2:8], squares.rearrange("p (h d) -> p h d", d=HD), AXX, ALU.add))
                    dve.tensor_scalar(merge_ms[:, 0:1], merge_ms[:, 0:1], 1.0 / AW, EPS, ALU.mult, ALU.add)
                    dve.tensor_scalar(merge_ms[:, 1:2], merge_ms[:, 1:2], 1.0 / CW, EPS, ALU.mult, ALU.add)
                    dve.tensor_scalar(merge_ms[:, 2:8], merge_ms[:, 2:8], 1.0 / HD, EPS, ALU.mult,
                                      ALU.add).then_inc(merge_meansq, 1)
                    dve.wait_ge(merge_rooted, l * T + t + 1)
                    step.after(dve.reciprocal(merge_root[:], merge_root[:]))
                    dve.scalar_tensor_tensor(out=ya, in0=ya, scalar=merge_root[:, 0:1], in1=pcol("out_norm_a"),
                                             op0=ALU.mult, op1=ALU.mult)
                    dve.scalar_tensor_tensor(out=yc, in0=yc, scalar=merge_root[:, 1:2], in1=pcol("out_norm_c"),
                                             op0=ALU.mult, op1=ALU.mult)
                    step.after(dve.tensor_tensor(yb_heads, yb_heads,
                                                 merge_root[:, 2:8].unsqueeze(2).broadcast_to(yb_heads.shape), ALU.mult))
                    dve.scalar_tensor_tensor(out=yb_heads, in0=yb_heads, scalar=pcol("depth")[:, 1:2],
                                             in1=pcol("subln_g").unsqueeze(1).broadcast_to(yb_heads.shape),
                                             op0=ALU.mult, op1=ALU.mult).then_inc(merged_ready, 1)

                for i in range(OUT_CHUNKS * T):
                    n, t = i // T, i % T
                    dve.wait_ge(out_copied, l * OUT_CHUNKS * T + i + 1)
                    part = merged[:, (i % 2) * NB:(i % 2 + 1) * NB]
                    to = x[:, t, n * NB:(n + 1) * NB]
                    step.after(dve.tensor_tensor(part, part, ps_mb[:, (i % 2) * NB:(i % 2 + 1) * NB], ALU.mult))
                    dve.tensor_tensor(to, to, part, ALU.add).then_inc(x_mixed, 1)

                norm(1)

                for i in range(16):
                    dve.wait_ge(ps_done, l * 16 + i + 1)
                    h, c = i // 2, i % 2
                    to = peer_scores.rearrange("p (t h) m -> p t h m", t=T)[:, :, h, c * N_KEYS:(c + 1) * N_KEYS]
                    dve.tensor_copy(to, tr(i, T * P).rearrange("p (t n) -> p t n", t=T)).then_inc(ps_ready, 1)
                dve.wait_ge(ps_ready, (l + 1) * 16)

                def route(m, where, p):
                    step.before_search(dve.tensor_copy(st[:], peer_scores[:, where, :]))
                    for lo, src in ((0, st), (8, st_rest)):
                        for c in range(2):
                            last = dve.max(half_top[:, c, lo:lo + 8], src[:, c * N_KEYS:(c + 1) * N_KEYS])
                        step.before_search(last)
                        for c in range(2):
                            half = src[:, c * N_KEYS:(c + 1) * N_KEYS]
                            last = dve.max_index(half_idx[:, c, lo:lo + 8], half_top[:, c, lo:lo + 8], half)
                        if lo == 0:
                            for c in range(2):
                                half = src[:, c * N_KEYS:(c + 1) * N_KEYS]
                                last = dve.match_replace(st_rest[:, c * N_KEYS:(c + 1) * N_KEYS], half_top[:, c, 0:8], half, NEG)
                        step.before_search(last)
                    dve.tensor_copy(half_idx_f[:], half_idx[:])
                    step.before_search(dve.tensor_tensor(cand[:], half_top[:, 0].unsqueeze(2).broadcast_to(cand.shape),
                                                 half_top[:, 1].unsqueeze(1).broadcast_to(cand.shape), ALU.add))
                    flat = cand[:].rearrange("p a b -> p (a b)")
                    step.before_search(dve.max(pair_top[:, p, 0:8], flat))
                    dve.max_index(pair_pos[:, 0:8], pair_top[:, p, 0:8], flat)
                    step.before_search(dve.match_replace(st[:], pair_top[:, p, 0:8], flat, NEG))
                    step.before_search(dve.max(pair_top[:, p, 8:16], st[:]))
                    dve.tensor_scalar(pair_neg[:, p:p + 1], pair_top[:, p, 0:1], -1.0, None, ALU.mult).then_inc(gate_max, 1)
                    step.after(dve.max_index(pair_pos[:, 8:16], pair_top[:, p, 8:16], st[:]))
                    dve.tensor_scalar(pair_ab[:, 0], pair_pos[:], 4, None, ALU.logical_shift_right)
                    step.after(dve.tensor_scalar(pair_ab[:, 1], pair_pos[:], TOPK - 1, None, ALU.bitwise_and))
                    step.after(dve.tensor_copy(pair_ab_f[:], pair_ab[:]))
                    hit = (cand[:], st_rest[:].rearrange("p (a b) -> p a b", a=TOPK))
                    for c in range(2):
                        last = dve.tensor_tensor(hit[c], iota16.unsqueeze(1).broadcast_to(cand.shape),
                                                 pair_ab_f[:, c].unsqueeze(2).broadcast_to(cand.shape), ALU.is_equal)
                    step.after(last)
                    for c in range(2):
                        last = dve.tensor_tensor(hit[c], hit[c], half_idx_f[:, c].unsqueeze(1).broadcast_to(cand.shape), ALU.mult)
                    step.after(last)
                    for c in range(2):
                        last = dve.tensor_reduce(pair_key[:, c], hit[c], AXX, ALU.add)
                    step.after(last)
                    step.after(dve.scalar_tensor_tensor(out=idx_f[:], in0=pair_key[:, 0], scalar=float(N_KEYS), in1=pair_key[:, 1],
                                                        op0=ALU.mult, op1=ALU.add))
                    dve.wait_ge(expert_taken, m + 1)
                    dve.tensor_scalar(expert[:, p, :], idx_f[:], layer_base[:], None, ALU.add).then_inc(expert_ready, 1)

                def dot(m, t, p):
                    for k in range(TOPK):
                        dve.wait_ge(u_full[k], (m + 1) * 16)
                        row = u_ring[:, k, :]
                        dve.tensor_tensor_reduce(row, row, h2[:, t, :], 1.0, 0.0, ALU.mult, ALU.add,
                                                 dots[:, p, k:k + 1]).then_inc(u_used, 1)
                    dve.wait_ge(u_used, (m + 1) * TOPK + URING)
                    a, q = dots[:, p, :], poly[:, p, :]
                    step.after(dve.tensor_tensor(q, a, a, ALU.mult))
                    step.after(dve.tensor_scalar(q, q, GELU_A, 1.0, ALU.mult, ALU.add))
                    step.after(dve.tensor_tensor(q, q, a, ALU.mult))
                    dve.tensor_scalar(q, q, -50.0, None, ALU.max).then_inc(poly_ready, 1)
                    dve.wait_ge(gate_exp, m + 1)
                    step.after(dve.reciprocal(gate_inv[:], gate_sum[:, p:p + 1]))
                    step.after(dve.scalar_tensor_tensor(out=act_work[:], in0=a, scalar=gate_inv[:], in1=gate[:, p, :],
                                                        op0=ALU.mult, op1=ALU.mult))
                    dve.wait_ge(gexp_ready, m + 1)
                    step.after(dve.tensor_scalar(gexp[:], gexp[:], 1.0, None, ALU.add))
                    step.after(dve.reciprocal(gexp[:], gexp[:]))
                    dve.tensor_tensor(coef[:, p, :], act_work[:], gexp[:], ALU.mult).then_inc(coef_ready, 1)

                def feed(t):
                    dve.wait_ge(acc_copied, l * T + t + 1)
                    step.after(dve.tensor_tensor(h2[:, t, :], h2[:, t, :], ps_mb[:], ALU.mult))
                    last = dve.tensor_tensor(x[:, t, :], x[:, t, :], h2[:, t, :], ALU.add).then_inc(x_fed, 1)
                    return last

                route(l * NH, 0, 0)
                layer_steps = step
                for t in range(T):
                    def pair(s, i, last=False):
                        m = l * NH + t * P_HEADS + i * 2
                        where = t * P_HEADS + i * 2
                        route(m + 1, where + 1, 1)
                        dot(m, t, 0)
                        if not last:
                            route(m + 2, where + 2, 0)
                        dot(m + 1, t, 1)

                    trips = P_HEADS // 2 - (t == T - 1)
                    with dve.Fori(0, trips) as i:
                        step = Steps(dve, dve_step, search_may)
                        step.base = layer_steps.base + layer_steps.n + i * link_counts["pair"]
                        pair(step, i)
                        assert step.n == link_counts["pair"], ("pair", step.n)
                    layer_steps.n += trips * link_counts["pair"]
                    step = layer_steps
                    if t == T - 1:
                        pair(step, P_HEADS // 2 - 1, last=True)
                    if t:
                        feed(t - 1)
                feed(T - 1)
                dve.wait_ge(x_fed, (l + 1) * T)
                dve.sem_inc(layer_done, 1)
                assert step.n == link_counts["layer"], ("layer", step.n)
            step.base = 0


def rope_tables():
    tokens = np.arange(2 * P)
    parts = []
    for dim in (HD, DK):
        quarter = dim // 4
        inv = np.float32(ROPE_BASE) ** (-np.arange(quarter, dtype=np.float32) / np.float32(quarter))
        cos, sin = [], []
        for pos in (tokens // GRID_W, tokens % GRID_W):
            angle = pos.astype(np.float32)[:, None] * inv
            cos += [np.cos(angle)] * 2
            sin += [-np.sin(angle), np.sin(angle)]
        parts += [np.concatenate(cos, 1), np.concatenate(sin, 1)]
    return np.concatenate(parts, 1).astype(np.float32)


def shape_constants():
    const = np.zeros((P, N_CONST), np.float32)
    const[:, C_ID:C_ID + P] = np.eye(P)
    const[:, C_IOTA:C_IOTA + TOPK] = np.arange(TOPK)
    const[:, C_EPS] = EPS
    for c in range(2):
        const[c, C_SEL + c * P:C_SEL + (c + 1) * P] = 1.0
    dense = np.zeros((P, N_DENSE), np.float32)
    dense[:, D_DOWN:D_DOWN + P] = np.eye(P, k=1)
    dense[:, D_UP:D_UP + P] = np.eye(P, k=-1)
    dense[P - 1, D_EPREV] = 1.0
    dense[0, D_ENEXT + P - 1] = 1.0
    rope = rope_tables()
    dense[:, D_ROPE:D_ROPE + ROPE_W] = rope[0:P]
    dense[:, D_ROPE + ROPE_W:] = rope[P:]
    depth = np.zeros((DEPTH, 4), np.float32)
    for l in range(DEPTH):
        lam_init = 0.8 - 0.6 * np.exp(-0.3 * l)
        depth[l] = lam_init, 1.0 - lam_init, l * N_EXPERTS, 0.0
    return const, dense, depth


LINKS = {"layer": 718, "pair": 46}


def kernel(**inputs):
    import concourse.bacc as bacc
    from concourse.bass_utils import run_bass_kernel_spmd

    a = {k: np.ascontiguousarray(v) for k, v in inputs.items()}
    const, dense, depth = shape_constants()
    packed = {"depth": depth}
    for name in PARAMS:
        if name != "depth":
            packed[name] = a[name].reshape(DEPTH, -1)
    arrays = {n: a[n] for n in ("x_prompt", "x_sample", "cache_a_k", "cache_a_v", "cache_b_k", "cache_b_v")}
    arrays["cond"] = np.concatenate([a["c"].reshape(1, DM), a["c_ctx"].reshape(1, DM)])
    arrays["ada_w"], arrays["ada_b"] = a["ada_w"], a["ada_b"]
    arrays["norm_g"] = np.concatenate([a["norm1_g"], a["norm2_g"]], axis=1)
    arrays["w_in"] = a["w_in"]
    arrays["params"] = np.concatenate([packed[n] for n in PARAMS], axis=1)
    arrays["w_out"], arrays["peer_wq"] = a["w_out"], a["peer_wq"]
    arrays["peer_keys"] = np.ascontiguousarray(a["peer_keys"].transpose(0, 4, 1, 2, 3)).reshape(DEPTH, P, -1)
    arrays["peer_u"] = a["peer_u"].reshape(DEPTH * N_EXPERTS, DM)
    arrays["peer_v"] = a["peer_v"].reshape(DEPTH * N_EXPERTS, DM)
    arrays["const"], arrays["dense_const"] = const, dense
    outs = {"y_prompt": (1, P, DM), "y_sample": (1, 2 * P, DM),
            "new_a_k": (1, DEPTH, P, A_KV, HD), "new_a_v": (1, DEPTH, P, A_KV, HD),
            "new_b_k": (1, DEPTH, P, B_HEADS, 2, DK), "new_b_v": (1, DEPTH, P, B_HEADS, HD)}
    nc = bacc.Bacc("TRN2", target_bir_lowering=False, num_devices=1)
    aps = {n: nc.dram_tensor(n, v.shape, mybir.dt.from_np(v.dtype), kind="ExternalInput").ap() for n, v in arrays.items()}
    aps |= {n: nc.dram_tensor(n, s, F32, kind="ExternalOutput").ap() for n, s in outs.items()}
    build(nc, **aps, link_counts=LINKS)
    r = run_bass_kernel_spmd(nc, [arrays], core_ids=[0])
    return tuple(r.results[0][n] for n in outs)
```

```python
from contextlib import ExitStack

import numpy as np

import concourse.bass as bass
from concourse import mybir

F32 = mybir.dt.float32
U32 = mybir.dt.uint32
ALU = mybir.AluOpType
ACT = mybir.ActivationFunctionType
AXX = mybir.AxisListType.X

P = 128
DM = 1024
KC = DM // P
DEPTH = 2
T = 3
COND = (1, 0, 0)
P_TILES, S_TILES = (0,), (1, 2)
EPS = 1e-6
HD, DK = 64, 32
A_HEADS, A_KV, B_HEADS, CW = 6, 2, 6, 256
AW, BW = A_HEADS * HD, B_HEADS * HD
QA, KA, VA = 0, AW, AW + A_KV * HD
QB = VA + A_KV * HD
KB, VB = QB + BW, QB + 2 * BW
CI = VB + BW
CB, CC = CI + CW, CI + 2 * CW
DPROJ = CC + CW
GA, GB = (VA - QA) // HD, (VB - QB) // DK
N_KEYS = 128
P_HEADS, TOPK = 8, 16
N_EXPERTS = N_KEYS * N_KEYS
NH = T * P_HEADS
GRID_W, ROPE_BASE = 64, 10000.0
PAST = 128

NB = 512
ADA_CHUNKS = 6 * DM // NB
IN_CHUNKS = DPROJ // NB
OUT_CHUNKS = DM // NB
Q_CHUNKS = P_HEADS * 2 * P // NB
C_IN = 0
C_OUT = C_IN + IN_CHUNKS
C_KEYS = C_OUT + OUT_CHUNKS
C_Q = C_KEYS + 1
GROUP_CHUNKS = C_Q + Q_CHUNKS
LAYER_CHUNKS = ADA_CHUNKS + 2 * GROUP_CHUNKS
WRING = 2
GROUP = 4
STEPS = TOPK // GROUP
URING = VRING = DRING = 2 * GROUP
ROWS = 12
UNITS = A_HEADS + 2 * B_HEADS
HEADS = A_HEADS + B_HEADS
W_MOD, W_NORM, W_PROJ, W_QK, W_KEYS_T, W_HEAD, W_TILE, W_OUT = 7, 7, 7, 4, 2, 6, 8, 7
QK_PARTS = 4


def mod_weight():
    return ADA_CHUNKS * W_MOD + W_QK


def dense_weight(tiles):
    a_tile = 2 * W_NORM + IN_CHUNKS * W_PROJ + QK_PARTS * W_QK + 2 * W_TILE + HEADS * W_HEAD + OUT_CHUNKS * W_OUT
    slots = 1 if tiles == P_TILES else 3
    return len(tiles) * a_tile + slots * W_KEYS_T + W_QK + 16 * 2 * len(tiles)


GELU_A = 0.044715
GELU_B = float(np.sqrt(2.0 / np.pi))
NEG = -3.0e38

PARAMS = {}
_at = 0
for _name, _n in (("qn_a", HD), ("kn_a", HD), ("qn_b", DK), ("kn_b", DK), ("lam_q1", DK), ("lam_k1", DK),
                  ("lam_q2", DK), ("lam_k2", DK), ("subln_g", HD), ("out_norm_a", AW), ("out_norm_c", CW),
                  ("conv_w", 3 * CW), ("conv_b", CW), ("depth", 4)):
    PARAMS[_name] = (_at, _at + _n)
    _at += _n
N_PARAMS = _at

C_ZERO, C_ID, C_IOTA, C_EPS, C_PLUS = 0, P, 3 * P, 3 * P + TOPK, 3 * P + TOPK + 1
N_CONST = C_PLUS + 1
ROPE_W = 2 * HD + 2 * DK
N_DENSE = 2 * ROPE_W
SHIFT1, GAIN1, GATE1, SHIFT2, GAIN2, GATE2 = range(6)


class Steps:

    def __init__(self, engine, sem, base=0, search_may=None):
        self.engine, self.sem, self.base, self.n = engine, sem, base, 0
        self.search_may = search_may

    def after(self, ins):
        self.n += 1
        ins.then_inc(self.sem, 1)
        self.engine.wait_ge(self.sem, self.base + self.n)

    def before_search(self, ins):
        self.after(ins)
        self.engine.sem_inc(self.search_may, 1)


class Beside:

    def __init__(self, program, weight, steps, first=2):
        self.program, self.weight, self.share = program, weight, weight / (GROUP * (steps - first - 2))
        self.wait, self.due, self.done = first * GROUP, 0.0, 0

    def quarter(self):
        if self.wait:
            self.wait -= 1
            return
        self.due += self.share
        while self.done < self.due - 1e-6 and self.done < self.weight:
            self.done += next(self.program)

    def step(self):
        for _ in range(GROUP):
            self.quarter()

    def end(self):
        for w in self.program:
            self.done += w
        assert self.done == self.weight, (self.done, self.weight)


def nothing():
    return Beside(iter(()), 0, 3)


def build(nc, x_prompt, x_sample, cache_a_k, cache_a_v, cache_b_k, cache_b_v, cond, ada_w, ada_b, norm_g,
          w_in, params, w_out, peer_wq, peer_keys, peer_u, peer_v, const, dense_const,
          y_prompt, y_sample, new_a_k, new_a_v, new_b_k, new_b_v):
    with ExitStack() as ctx:
        def sb(name, shape, dt=F32):
            return ctx.enter_context(nc.sbuf_tensor(name, shape, dt))

        def psum(name):
            return ctx.enter_context(nc.psum_tensor(name, [P, 2 * NB], F32))

        def sem(name):
            return ctx.enter_context(nc.semaphore(name))

        x = sb("x", [P, T, DM])
        consts = sb("consts", [P, N_CONST])
        ident = consts[:, C_ID:C_ID + P]
        zeros = consts[:, C_ZERO:C_ZERO + P]
        iota16 = consts[:, C_IOTA:C_IOTA + TOPK]
        eps = consts[:, C_EPS:C_EPS + 1]
        condT = sb("condT", [P, KC, 2])
        mods = sb("mods", [P, DM])
        weights = sb("weights", [P, WRING, KC, NB])
        u_ring = sb("u_ring", [P, URING, DM])
        v_ring = sb("v_ring", [P, VRING, DM])
        hT = sb("hT", [P, KC, 2 * P])
        par = sb("par", [P, N_PARAMS])
        dense = sb("dense", [P, N_DENSE])
        scratch = sb("scratch", [P, VB])
        merged = sb("merged", [P, DM])
        proj_buf = sb("proj", [P, 2 * DPROJ])
        proj = proj_buf[:].rearrange("p (t n) -> p t n", t=2)
        keysT = proj_buf[:, 0:2 * P_HEADS * P].rearrange("p (i n) -> p i n", n=P)
        pqT = proj_buf[:, 2 * P_HEADS * P:2 * P_HEADS * P + 4 * 2 * P].rearrange("p (r n) -> p r n", r=4)
        scores_buf = sb("scores", [P, NH * 2 * N_KEYS])
        peer_scores = scores_buf[:].rearrange("p (n m) -> p n m", m=2 * N_KEYS)
        h2 = sb("h2", [P, T, DM])
        h2_flat = h2[:].rearrange("p t d -> p (t d)")

        class Work:

            def __init__(self, tiles):
                n, first = len(tiles), tiles[0]
                self.slots = slots = 1 if n == 1 else 3
                self.at = first * P_HEADS * 2 * N_KEYS
                self.h_at = first * DM
                self.probs = self.take(5 * slots * P).rearrange("p (r n) -> p r n", r=5)
                self.probsT = self.take(2 * slots * P).rearrange("p (r n) -> p r n", r=2)
                self.conv_u = proj[:, 0:n, CI:CB]
                if n == 1:
                    kT = self.take(4 * P)
                    self.qT = self.take_h(6 * P)
                else:
                    self.past_va = self.take(P)
                    self.past_vb = self.take(BW)
                    self.qT = self.take(6 * P)
                    kT = self.take_h(4 * slots * P)
                    self.past_ka = self.take_h(P)
                    self.past_kb = self.take_h(BW)
                self.qT = self.qT.rearrange("p (c n) -> p c n", c=6)
                self.kT = kT.rearrange("p (c j n) -> p c j n", c=4, j=slots)
                assert self.at <= (first + n) * P_HEADS * 2 * N_KEYS and self.h_at <= (first + n) * DM

            def take(self, n):
                self.at += n
                return scores_buf[:, self.at - n:self.at]

            def take_h(self, n):
                self.h_at += n
                return h2_flat[:, self.h_at - n:self.h_at]

        work_of = {P_TILES: Work(P_TILES), S_TILES: Work(S_TILES)}

        sumsq = sb("sumsq", [P, 4])
        rstd = sb("rstd", [P, 4])
        qk_ms = sb("qk_ms", [P, 2, GA + GB])
        qk_root = sb("qk_root", [P, 2, GA + GB])
        rowmax = sb("rowmax", [P, UNITS])
        negmax = sb("negmax", [P, UNITS])
        rowsum = sb("rowsum", [P, UNITS])
        rinv = sb("rinv", [P, UNITS])
        merge_ms = sb("merge_ms", [P, 8])
        merge_root = sb("merge_root", [P, 8])
        lam_work = sb("lam_work", [P, 8])
        layer_base = sb("layer_base", [P, 2])
        cond_work = sb("cond_work", [P, 2, KC, 2])
        st = sb("st", [P, 2 * N_KEYS])
        st_rest = sb("st_rest", [P, 2 * N_KEYS])
        cand = sb("cand", [P, TOPK, TOPK])
        half_top = sb("half_top", [P, 2, TOPK])
        half_idx = sb("half_idx", [P, 2, TOPK], U32)
        half_idx_f = sb("half_idx_f", [P, 2, TOPK])
        pair_top = sb("pair_top", [P, 2, TOPK])
        pair_pos = sb("pair_pos", [P, TOPK], U32)
        pair_ab = sb("pair_ab", [P, 2, TOPK], U32)
        pair_ab_f = sb("pair_ab_f", [P, 2, TOPK])
        pair_key = sb("pair_key", [P, 2, TOPK])
        idx_f = sb("idx_f", [P, TOPK])
        expert = sb("expert", [P, 2, TOPK], U32)
        gathered = sb("gathered", [P, 2, TOPK], U32)
        pair_neg = sb("pair_neg", [P, 2])
        pair_exp = sb("pair_exp", [P, 2, TOPK])
        gate_sum = sb("gate_sum", [P, 2])
        gate_inv = sb("gate_inv", [P, 1])
        gate = sb("gate", [P, 2, TOPK])
        dots = sb("dots", [P, 2, TOPK])
        poly = sb("poly", [P, 2, TOPK])
        gexp = sb("gexp", [P, 2, GROUP])
        weighed = sb("weighed", [P, GROUP])
        coef = sb("coef", [P, 2, TOPK])
        diag = sb("diag", [P, DRING, P])

        ps_acc = psum("ps_acc")
        ps_mb = psum("ps_mb")
        ps_mm = psum("ps_mm")
        ps_tr = psum("ps_tr")

        def mm(i, n=NB):
            return ps_mm[:, (i % 2) * NB:(i % 2) * NB + n]

        def tr(i, n=NB):
            return ps_tr[:, (i % 2) * NB:(i % 2) * NB + n]

        const_loaded = sem("const_loaded")
        x_loaded = sem("x_loaded")
        w_full = [sem(f"w_full{i}") for i in range(WRING)]
        params_loaded = sem("params_loaded")
        mod_in_loaded = sem("mod_in_loaded")
        past_loaded = sem("past_loaded")
        cond_ready = sem("cond_ready")
        cond_exp = sem("cond_exp")
        mod_mm = sem("mod_mm")
        mod_staged = sem("mod_staged")
        mod_moved = [sem(f"mod_moved{i}") for i in range(2)]
        mod_ready = sem("mod_ready")
        rms_root = sem("rms_root")
        gain_bc = sem("gain_bc")
        shift_bc = sem("shift_bc")
        h_ready = sem("h_ready")
        h_mm = sem("h_mm")
        hT_ready = sem("hT_ready")
        proj_mm = sem("proj_mm")
        proj_ready = sem("proj_ready")
        qk_meansq = sem("qk_meansq")
        qk_rooted = sem("qk_rooted")
        kv_ready = sem("kv_ready")
        kv_stored = sem("kv_stored")
        qk_ready = sem("qk_ready")
        lam_sums = sem("lam_sums")
        lam_exps = sem("lam_exps")
        kT_mm = sem("kT_mm")
        kT_ready = sem("kT_ready")
        qT_mm = sem("qT_mm")
        qT_ready = sem("qT_ready")
        score_mm = sem("score_mm")
        negmax_ready = sem("negmax_ready")
        exp_ready = sem("exp_ready")
        mix_ready = sem("mix_ready")
        pT_mm = sem("pT_mm")
        pT_ready = sem("pT_ready")
        pv_done = sem("pv_done")
        conv_mm = sem("conv_mm")
        conv_read = sem("conv_read")
        merge_meansq = sem("merge_meansq")
        merge_rooted = sem("merge_rooted")
        merged_ready = sem("merged_ready")
        mergedT_mm = sem("mergedT_mm")
        mergedT_ready = sem("mergedT_ready")
        out_mm = sem("out_mm")
        out_copied = sem("out_copied")
        x_mixed = sem("x_mixed")
        keys_ready = sem("keys_ready")
        pq_mm = sem("pq_mm")
        pq_ready = sem("pq_ready")
        ps_done = sem("ps_done")
        ps_ready = sem("ps_ready")
        expert_ready = sem("expert_ready")
        expert_taken = sem("expert_taken")
        gate_max = sem("gate_max")
        gate_exp = sem("gate_exp")
        u_full = [sem(f"u_full{k}") for k in range(URING)]
        u_used = sem("u_used")
        v_full = [sem(f"v_full{k}") for k in range(VRING)]
        v_used = sem("v_used")
        poly_ready = sem("poly_ready")
        gexp_ready = sem("gexp_ready")
        coef_ready = sem("coef_ready")
        diag_ready = sem("diag_ready")
        acc_done = sem("acc_done")
        acc_copied = sem("acc_copied")
        gate2_bc = sem("gate2_bc")
        x_fed = sem("x_fed")
        y_stored = sem("y_stored")
        gather_may = sem("gather_may")
        search_may = sem("search_may")
        dve_step = sem("dve_step")
        act_step = sem("act_step")

        block = ctx.enter_context(nc.Block())

        def pcol(name):
            a, b = PARAMS[name]
            return par[:, a:b]

        def probs_slot(head, second=0):
            return 3 + head % 2 if second else head % 3

        def units(head):
            return (head,) if head < A_HEADS else (2 * head - A_HEADS, 2 * head - A_HEADS + 1)

        def nth(l, tiles, per, i):
            return (l * T + tiles[0]) * per + i + 1

        def group_nth(l, tiles, i=0, per=1):
            return (l * 2 + (tiles == S_TILES)) * per + i + 1

        def slot_nth(l, tiles, i):
            return l * 4 + (tiles == S_TILES) + i + 1

        def first_chunk(l, tiles=None):
            if tiles is None:
                return l * LAYER_CHUNKS
            return l * LAYER_CHUNKS + ADA_CHUNKS + (tiles == S_TILES) * GROUP_CHUNKS

        def first_head(l, tiles):
            return l * NH + tiles[0] * P_HEADS

        @block.sync
        def _(sp):
            with nc.allow_non_contiguous_dma("the conditioning vectors, 8 KB"):
                for c in range(2):
                    sp.dma_start(cond_work[:, 0, :, c], cond[c].rearrange("(k p) -> p k", p=P)).then_inc(const_loaded, 16)
            sp.dma_start(consts[:], const).then_inc(const_loaded, 16)

            def used(c):
                l, c = c // LAYER_CHUNKS, c % LAYER_CHUNKS
                if c < ADA_CHUNKS:
                    return mod_mm, l * ADA_CHUNKS + c + 1
                tiles = P_TILES if c < ADA_CHUNKS + GROUP_CHUNKS else S_TILES
                c, n = (c - ADA_CHUNKS) % GROUP_CHUNKS, len(tiles)
                if c < C_OUT:
                    return proj_mm, nth(l, tiles, IN_CHUNKS, (c - C_IN + 1) * n - 1)
                if c < C_KEYS:
                    return out_mm, nth(l, tiles, OUT_CHUNKS, (c - C_OUT + 1) * n - 1)
                if c == C_KEYS:
                    return keys_ready, group_nth(l, tiles)
                return pq_mm, group_nth(l, tiles, (c - C_Q + 1) * 4 - 1, 16)

            def chunk(c, src):
                if c >= WRING:
                    sp.wait_ge(*used(c - WRING))
                dst = weights[:, c % WRING, :, :]
                if len(src.shape) == 2:
                    dst = dst.rearrange("p k n -> p (k n)")[:, 0:2 * P_HEADS * P]
                sp.dma_start(dst, src).then_inc(w_full[c % WRING], 16)

            def columns(w, n):
                return w.rearrange("(k p) n -> p k n", p=P)[:, :, n * NB:(n + 1) * NB]

            def past(l):
                if l:
                    sp.wait_ge(x_fed, l * T)
                w = work_of[S_TILES]
                sp.dma_start(w.past_ka, cache_a_k[0, l].rearrange("s k d -> s (k d)")).then_inc(past_loaded, 16)
                sp.dma_start(w.past_va, cache_a_v[0, l].rearrange("s k d -> s (k d)")).then_inc(past_loaded, 16)
                sp.dma_start(w.past_kb, cache_b_k[0, l].rearrange("s h j d -> s (h j d)")).then_inc(past_loaded, 16)
                sp.dma_start(w.past_vb, cache_b_v[0, l].rearrange("s h d -> s (h d)")).then_inc(past_loaded, 16)

            def group_chunks(l, tiles):
                c = first_chunk(l, tiles)
                for n in range(IN_CHUNKS):
                    chunk(c + C_IN + n, columns(w_in[l], n))
                    if n == 1 and tiles == S_TILES:
                        past(l)
                for n in range(OUT_CHUNKS):
                    chunk(c + C_OUT + n, columns(w_out[l], n))
                chunk(c + C_KEYS, peer_keys[l])
                if tiles == P_TILES:
                    sp.wait_ge(kv_ready, l + 1)
                    sp.dma_start(new_a_k[0, l].rearrange("s k d -> s (k d)"), proj[:, 0, KA:VA]).then_inc(kv_stored, 16)
                    sp.dma_start(new_a_v[0, l].rearrange("s k d -> s (k d)"), proj[:, 0, VA:QB]).then_inc(kv_stored, 16)
                    sp.dma_start(new_b_k[0, l].rearrange("s h j d -> s (h j d)"), proj[:, 0, KB:VB]).then_inc(kv_stored, 16)
                    sp.dma_start(new_b_v[0, l].rearrange("s h d -> s (h d)"), proj[:, 0, VB:CI]).then_inc(kv_stored, 16)
                for n in range(Q_CHUNKS):
                    chunk(c + C_Q + n, columns(peer_wq[l], n))

            for l in range(DEPTH):
                c = first_chunk(l)
                for n in range(ADA_CHUNKS):
                    chunk(c + n, columns(ada_w[l], n))
                    if n == 1:
                        if l:
                            sp.wait_ge(ps_done, group_nth(l - 1, S_TILES, 15, 16))
                        rows = slice(32 * l, 32 * l + ROWS)
                        sp.dma_start(proj_buf[rows, 0:DM], ada_b[l]).then_inc(mod_in_loaded, 16)
                        sp.dma_start(proj_buf[rows, DM:2 * DM], norm_g[l]).then_inc(mod_in_loaded, 16)
                        sp.dma_start(par[:], params[l:l + 1, :].partition_broadcast(P).rearrange("p o n -> p (o n)")).then_inc(params_loaded, 16)
                        sp.dma_start(dense[:], dense_const).then_inc(params_loaded, 16)
                        if l == 0:
                            sp.dma_start(x[:, 0, :], x_prompt[0]).then_inc(x_loaded, 16)
                            sp.dma_start(x[:, 1:3, :], x_sample[0].rearrange("(t p) d -> p t d", p=P)).then_inc(x_loaded, 16)
                group_chunks(l, P_TILES)
                group_chunks(l, S_TILES)
            sp.wait_ge(x_fed, (DEPTH - 1) * T + 1)
            sp.dma_start(y_prompt[0], x[:, 0, :]).then_inc(y_stored, 16)
            sp.wait_ge(x_fed, DEPTH * T)
            sp.dma_start(y_sample[0].rearrange("(t p) d -> p t d", p=P), x[:, 1:3, :]).then_inc(y_stored, 16)
            sp.wait_ge(y_stored, 32)
            sp.wait_ge(kv_stored, DEPTH * 64)

        @block.gpsimd
        def _(pool):
            pool.sem_inc(expert_taken, 2)

            def take(n, p):
                pool.wait_ge(expert_ready, n + 1)
                pool.sem_inc(gather_may, 1)
                pool.tensor_copy(gathered[:, p, :], expert[:, p, :]).then_inc(expert_taken, 1)
                pool.wait_ge(expert_taken, n + 3)
                pool.sem_inc(gather_may, 1)

            def gather(ring, full, used, table, n, p, g):
                for k in range(GROUP):
                    slot = (g % 2) * GROUP + k
                    pool.wait_ge(used, n * TOPK + g * GROUP + k + 1)
                    pool.sem_inc(gather_may, 1)
                    at = g * GROUP + k
                    pool.indirect_dma_start(
                        ring[:, slot, :], None, table,
                        bass.IndirectOffsetOnAxis(ap=gathered[:, p, at:at + 1], axis=0)).then_inc(full[slot], 16)

            def head(n, p, last=False):
                for g in range(STEPS):
                    if g + 1 < STEPS:
                        gather(u_ring, u_full, u_used, peer_u, n, p, g + 1)
                    elif not last:
                        take(n + 1, 1 - p)
                        gather(u_ring, u_full, u_used, peer_u, n + 1, 1 - p, 0)
                    gather(v_ring, v_full, v_used, peer_v, n, p, g)

            take(0, 0)
            gather(u_ring, u_full, u_used, peer_u, 0, 0, 0)
            with pool.Fori(0, DEPTH * NH // 2 - 1) as i:
                head(i * 2, 0)
                head(i * 2 + 1, 1)
            head(DEPTH * NH - 2, 0)
            head(DEPTH * NH - 1, 1, last=True)

        @block.tensor
        def _(pe):
            pe.sem_inc(v_used, VRING)
            pe.wait_ge(const_loaded, 3 * 16)
            pe.wait_ge(cond_ready, 1)

            def arrived(c):
                pe.wait_ge(w_full[c % WRING], (c // WRING + 1) * 16)
                return weights[:, c % WRING]

            def broadcast(out, l, t, part, n0=0, n=2):
                b = 32 * l
                r = b + 6 * COND[t] + part
                pick = consts[b:b + ROWS, C_ID + r:C_ID + r + 1].broadcast_to([ROWS, P])
                for i in range(n):
                    last = pe.matmul(out[:, i * NB:(i + 1) * NB], pick, mods[b:b + ROWS, (n0 + i) * NB:(n0 + i + 1) * NB],
                                     start=True, stop=True, tile_position=(b, 0))
                return last

            def shift(d):
                return consts[:, C_ID - d:C_ID - d + P]

            def modulate(l):
                for n in range(ADA_CHUNKS):
                    w = arrived(first_chunk(l) + n)
                    if n >= 2:
                        pe.wait_ge(mod_staged, l * ADA_CHUNKS + n - 1)
                    for k in range(KC):
                        last = pe.matmul(mm(n)[0:2, :], condT[:, k, :], w[:, k, :], start=(k == 0), stop=(k == KC - 1))
                    last.then_inc(mod_mm, 1)
                    yield W_MOD
                yield W_QK

            def norm(l, tiles, stage):
                for j, t in enumerate(tiles):
                    i = stage * len(tiles) + j
                    broadcast(ps_mb[:], l, t, (GAIN1, GAIN2)[stage]).then_inc(gain_bc, 1)
                    broadcast(ps_mm[:], l, t, (SHIFT1, SHIFT2)[stage]).then_inc(shift_bc, 1)
                    pe.wait_ge(h_ready, nth(l, tiles, 2, i))
                    if j:
                        pe.wait_ge(hT_ready, nth(l, tiles, 2, i - 1))
                    src = merged[:] if stage == 0 else h2[:, t, :]
                    for k in range(KC):
                        last = pe.transpose(ps_tr[:, k * P:(k + 1) * P], src[:, k * P:(k + 1) * P], ident)
                    last.then_inc(h_mm, 1)
                    yield W_NORM

            def dense_stages(l, tiles):
                w_, nt = work_of[tiles], len(tiles)
                nk = w_.slots
                chunk0 = first_chunk(l, tiles)
                pe.wait_ge(mod_ready, l + 1)
                if l or tiles == S_TILES:
                    pe.wait_ge(ps_ready, group_nth(l, tiles, -1, 16))
                pe.wait_ge(mod_staged, (l + 1) * ADA_CHUNKS)
                yield from norm(l, tiles, 0)
                pe.wait_ge(hT_ready, nth(l, tiles, 2, nt - 1))

                for n in range(IN_CHUNKS):
                    w = arrived(chunk0 + C_IN + n)
                    for j in range(nt):
                        i = n * nt + j
                        if i >= 2:
                            pe.wait_ge(proj_ready, nth(l, tiles, IN_CHUNKS, i - 2))
                        for k in range(KC):
                            last = pe.matmul(mm(i), hT[:, k, j * P:(j + 1) * P], w[:, k, :],
                                             start=(k == 0), stop=(k == KC - 1))
                        last.then_inc(proj_mm, 1)
                        yield W_PROJ
                for j in range(QK_PARTS * nt):
                    yield W_QK

                pe.wait_ge(qk_ready, group_nth(l, tiles))
                if tiles == S_TILES:
                    pe.wait_ge(past_loaded, (l + 1) * 64)
                for j in range(nk):
                    if j >= 2:
                        pe.wait_ge(kT_ready, slot_nth(l, tiles, j - 2))
                    ka = proj[:, j, KA:VA] if j < nt else w_.past_ka
                    kb = proj[:, j, KB:VB] if j < nt else w_.past_kb
                    pe.transpose(tr(j)[:, 0:P], ka, ident)
                    for c in range(3):
                        last = pe.transpose(tr(j)[:, (c + 1) * P:(c + 2) * P], kb[:, c * P:(c + 1) * P], ident)
                    last.then_inc(kT_mm, 1)
                    yield W_KEYS_T
                pe.wait_ge(kT_ready, slot_nth(l, tiles, nk - 1))

                for j, t in enumerate(tiles):
                    if j:
                        pe.wait_ge(merged_ready, nth(l, tiles, 1, j - 1))
                    down, up = shift(1), shift(-1)
                    pe.matmul(ps_mb[:, 0:CW], down, w_.conv_u[:, j, :], start=True, stop=(t != 2))
                    if t == 2:
                        pe.matmul(ps_mb[:, 0:CW], shift(1 - P), w_.conv_u[:, 0, :], start=False, stop=True)
                    last = pe.matmul(ps_mb[:, NB:NB + CW], up, w_.conv_u[:, j, :], start=True, stop=(t != 1))
                    if t == 1:
                        last = pe.matmul(ps_mb[:, NB:NB + CW], shift(P - 1), w_.conv_u[:, 1, :],
                                         start=False, stop=True)
                    last.then_inc(conv_mm, 1)
                    if j:
                        pe.wait_ge(mergedT_ready, nth(l, tiles, 1, j - 1))
                    for c in range(6):
                        col = QA + c * P if c < 3 else QB + (c - 3) * P
                        last = pe.transpose(ps_tr[:, c * P:(c + 1) * P], proj[:, j, col:col + P], ident)
                    last.then_inc(qT_mm, 1)
                    pe.wait_ge(qT_ready, nth(l, tiles, 1, j))

                    def scores(head):
                        for u in units(head):
                            g = j * UNITS + u
                            if g >= 2:
                                pe.wait_ge(exp_ready, nth(l, tiles, UNITS, g - 2))
                            m = u - A_HEADS
                            c, lo, n = (0, HD * (u // 3), HD) if u < A_HEADS else (1 + m // 4, DK * (m % 4), DK)
                            q = w_.qT[lo:lo + n, u % 3 if u < A_HEADS else 3 + m // 4, :]
                            k = w_.kT[lo:lo + n, c, :, :].rearrange("p j n -> p (j n)")
                            pe.matmul(mm(g, nk * P), q, k, start=True, stop=True, tile_position=(lo, 0)).then_inc(score_mm, 1)

                    def transpose_probs(head):
                        u = units(head)[0]
                        if head < A_HEADS:
                            pe.wait_ge(exp_ready, nth(l, tiles, UNITS, j * UNITS + u))
                        else:
                            pe.wait_ge(mix_ready, nth(l, tiles, B_HEADS, j * B_HEADS + head - A_HEADS))
                        if head >= 2:
                            pe.wait_ge(pT_ready, nth(l, tiles, HEADS, j * HEADS + head - 2))
                        for s in range(nk):
                            last = pe.transpose(tr(head)[:, s * P:(s + 1) * P], w_.probs[:, probs_slot(head), s * P:(s + 1) * P], ident)
                        last.then_inc(pT_mm, 1)

                    def weigh_values(head):
                        pe.wait_ge(pT_ready, nth(l, tiles, HEADS, j * HEADS + head))
                        if head == 0:
                            pe.wait_ge(conv_read, nth(l, tiles, 1, j))
                        for s in range(nk):
                            if head < A_HEADS:
                                col, kv = head * HD, (head // 3) * HD
                                v = proj[:, s, VA + kv:VA + kv + HD] if s < nt else w_.past_va[:, kv:kv + HD]
                            else:
                                hb = (head - A_HEADS) * HD
                                col = NB + hb
                                v = proj[:, s, VB + hb:VB + hb + HD] if s < nt else w_.past_vb[:, hb:hb + HD]
                            last = pe.matmul(ps_mb[:, col:col + HD], w_.probsT[:, head % 2, s * P:(s + 1) * P], v,
                                             start=(s == 0), stop=(s == nk - 1))
                        last.then_inc(pv_done, 1)

                    scores(0)
                    yield W_TILE
                    for head in range(HEADS):
                        if head + 1 < HEADS:
                            scores(head + 1)
                        if head >= 1:
                            transpose_probs(head - 1)
                        if head >= 2:
                            weigh_values(head - 2)
                        yield W_HEAD
                    transpose_probs(HEADS - 1)
                    weigh_values(HEADS - 2)
                    weigh_values(HEADS - 1)
                    pe.wait_ge(merged_ready, nth(l, tiles, 1, j))
                    pe.wait_ge(pT_ready, nth(l, tiles, HEADS, (j + 1) * HEADS - 1))
                    for k in range(KC):
                        last = pe.transpose(ps_tr[:, k * P:(k + 1) * P], merged[:, k * P:(k + 1) * P], ident)
                    last.then_inc(mergedT_mm, 1)
                    yield W_TILE

                pe.wait_ge(mergedT_ready, nth(l, tiles, 1, nt - 1))
                for n in range(OUT_CHUNKS):
                    w = arrived(chunk0 + C_OUT + n)
                    for j, t in enumerate(tiles):
                        i = n * nt + j
                        if i >= 2:
                            pe.wait_ge(x_mixed, nth(l, tiles, OUT_CHUNKS, i - 2))
                        for k in range(KC):
                            pe.matmul(mm(i), hT[:, k, j * P:(j + 1) * P], w[:, k, :], start=(k == 0), stop=(k == KC - 1))
                        broadcast(ps_mb[:, (i % 2) * NB:(i % 2 + 1) * NB], l, t, GATE1, n0=n, n=1).then_inc(out_mm, 1)
                        yield W_OUT

                pe.wait_ge(x_mixed, nth(l, tiles, OUT_CHUNKS, OUT_CHUNKS * nt - 1))
                yield from norm(l, tiles, 1)
                pe.wait_ge(hT_ready, nth(l, tiles, 2, 2 * nt - 1))

                pe.wait_ge(keys_ready, group_nth(l, tiles))
                yield W_QK

                def half_scores(i):
                    pe.wait_ge(pq_ready, group_nth(l, tiles, i, 16))
                    if i >= 2:
                        pe.wait_ge(ps_ready, group_nth(l, tiles, i - 2, 16))
                    for j in range(nt):
                        last = pe.matmul(tr(i)[:, j * P:(j + 1) * P], pqT[:, i % 4, j * P:(j + 1) * P], keysT[:, i, :],
                                         start=True, stop=True)
                    last.then_inc(ps_done, 1)

                for i in range(16):
                    if i % 4 == 0:
                        w = arrived(chunk0 + C_Q + i // 4)
                    if i >= 2:
                        pe.wait_ge(pq_ready, group_nth(l, tiles, i - 2, 16))
                    for k in range(KC):
                        last = pe.matmul(mm(i, nt * P), w[:, k, (i % 4) * P:(i % 4 + 1) * P], hT[:, k, 0:nt * P],
                                         start=(k == 0), stop=(k == KC - 1))
                    last.then_inc(pq_mm, 1)
                    if i:
                        half_scores(i - 1)
                    if i == 15:
                        half_scores(15)
                    yield 2 * nt

            def open_sum(tau):
                if tau:
                    pe.wait_ge(x_fed, tau)
                for n in range(2):
                    pe.matmul(ps_acc[:, n * NB:(n + 1) * NB], zeros, consts[:, 0:2 * P].unsqueeze(1).broadcast_to([P, 2, 2 * P]),
                              start=True, stop=False)

            def close_sum(l, t):
                for n in range(2):
                    last = pe.matmul(ps_acc[:, n * NB:(n + 1) * NB], zeros, consts[:, 0:2 * P].unsqueeze(1).broadcast_to([P, 2, 2 * P]),
                                     start=False, stop=True)
                last.then_inc(acc_done, 1)
                pe.wait_ge(acc_copied, l * T + t + 1)
                broadcast(ps_acc[:], l, t, GATE2).then_inc(gate2_bc, 1)

            def add_rows(n, g, side):
                for k in range(GROUP):
                    for _ in range(QUARTERS_BEFORE_ROW[k]):
                        side.quarter()
                    slot = (g % 2) * GROUP + k
                    pe.wait_ge(diag_ready, n * TOPK + g * GROUP + k + 1)
                    pe.wait_ge(v_full[slot], (n * 2 + g // 2 + 1) * 16)
                    for b in range(2):
                        last = pe.matmul(ps_acc[:, b * NB:(b + 1) * NB], diag[:, slot, :],
                                         v_ring[:, slot, b * NB:(b + 1) * NB], start=False, stop=False)
                    last.then_inc(v_used, 1)

            def experts(l, tiles, side):
                for t in tiles:
                    for s in range(P_HEADS * STEPS):
                        if t == tiles[-1] and s == P_HEADS * STEPS - 2:
                            side.end()
                            side = idle
                        if s == 0:
                            side.step()
                            continue
                        if s == 1:
                            open_sum(l * T + t)
                        add_rows(l * NH + t * P_HEADS + (s - 1) // STEPS, (s - 1) % STEPS, side)
                    add_rows(l * NH + (t + 1) * P_HEADS - 1, STEPS - 1, idle)
                    close_sum(l, t)

            idle = nothing()
            for _ in modulate(0):
                pass
            for _ in dense_stages(0, P_TILES):
                pass
            for l in range(DEPTH):
                experts(l, P_TILES, Beside(dense_stages(l, S_TILES), dense_weight(S_TILES), P_HEADS * STEPS))
                if l + 1 < DEPTH:
                    def next_layer():
                        yield from modulate(l + 1)
                        yield from dense_stages(l + 1, P_TILES)
                    experts(l, S_TILES, Beside(next_layer(), mod_weight() + dense_weight(P_TILES), NEXT_STEPS))
            l = DEPTH - 1
            for t in S_TILES:
                open_sum(l * T + t)
                with pe.Fori(0, P_HEADS // 2) as i:
                    for p in range(2):
                        for g in range(STEPS):
                            add_rows(l * NH + t * P_HEADS + p + i * 2, g, idle)
                close_sum(l, t)

        @block.scalar
        def _(act):
            step = Steps(act, act_step)
            act.wait_ge(const_loaded, 3 * 16)
            act.activation(cond_work[:, 1], cond_work[:, 0], ACT.Exp, scale=-1.0).then_inc(cond_exp, 1)

            def modulate(l):
                for n in range(ADA_CHUNKS):
                    half = merged[0:2, (n % 2) * NB:(n % 2 + 1) * NB]
                    act.wait_ge(mod_mm, l * ADA_CHUNKS + n + 1)
                    if l or n >= 2:
                        act.wait_ge(mod_moved[n % 2], (l * ADA_CHUNKS + n) // 2 * 16)
                    act.activation(half, mm(n)[0:2, :], ACT.Copy).then_inc(mod_staged, 1)
                    act.wait_ge(mod_staged, l * ADA_CHUNKS + n + 1)
                    row = 32 * l + n // 2
                    act.dma_start(mods[row:row + 7:6, (n % 2) * NB:(n % 2 + 1) * NB], half).then_inc(mod_moved[n % 2], 16)
                    yield W_MOD
                yield W_QK

            def norm(l, tiles, stage):
                for j, t in enumerate(tiles):
                    step.after(act.activation(scratch[:, 0:DM], x[:, t, :], ACT.Square, accum_out=sumsq[:, j:j + 1]))
                nt = len(tiles)
                act.activation(rstd[:, 0:nt], sumsq[:, 0:nt], ACT.Sqrt, bias=eps, scale=1.0 / DM).then_inc(rms_root, 1)
                for j in range(nt):
                    act.wait_ge(h_mm, nth(l, tiles, 2, stage * nt + j))
                    act.activation(hT[:, :, j * P:(j + 1) * P], ps_tr[:].rearrange("p (k n) -> p k n", k=KC),
                                   ACT.Copy).then_inc(hT_ready, 1)
                    yield W_NORM

            def dense_stages(l, tiles):
                w_, nt = work_of[tiles], len(tiles)
                nk = w_.slots
                if not l:
                    act.wait_ge(x_loaded, 2 * 16)
                if l:
                    for t in tiles:
                        act.wait_ge(x_fed, (l - 1) * T + t + 1)
                if l or tiles == S_TILES:
                    act.wait_ge(ps_ready, group_nth(l, tiles, -1, 16))
                yield from norm(l, tiles, 0)
                for n in range(IN_CHUNKS):
                    for j in range(nt):
                        i = n * nt + j
                        act.wait_ge(proj_mm, nth(l, tiles, IN_CHUNKS, i))
                        if i == 0:
                            act.wait_ge(mod_ready, l + 1)
                        if n == 0:
                            act.activation(proj[:, j, QA:KA].rearrange("p (r g d) -> p r g d", g=2, r=3),
                                           mm(i)[:, QA:KA].rearrange("p (g r d) -> p r g d", g=2, r=3), ACT.Copy)
                            act.activation(proj[:, j, KA:NB], mm(i)[:, KA:NB], ACT.Copy).then_inc(proj_ready, 1)
                        else:
                            act.activation(proj[:, j, n * NB:(n + 1) * NB], mm(i), ACT.Copy).then_inc(proj_ready, 1)
                        yield W_PROJ
                for j in range(nt - 1):
                    yield W_QK
                act.wait_ge(qk_meansq, group_nth(l, tiles))
                act.activation(qk_root[:, 0:nt], qk_ms[:, 0:nt], ACT.Sqrt).then_inc(qk_rooted, 1)
                if tiles == P_TILES:
                    act.wait_ge(lam_sums, l + 1)
                    act.activation(lam_work[:, 2:4], lam_work[:, 0:2], ACT.Exp).then_inc(lam_exps, 1)
                for j in range((QK_PARTS - 1) * nt + 1):
                    yield W_QK
                for j in range(nk):
                    act.wait_ge(kT_mm, slot_nth(l, tiles, j))
                    act.activation(w_.kT[:, :, j, :], tr(j).rearrange("p (c n) -> p c n", c=4), ACT.Copy).then_inc(kT_ready, 1)
                    yield W_KEYS_T
                for j in range(nt):
                    act.wait_ge(qT_mm, nth(l, tiles, 1, j))
                    act.activation(w_.qT, ps_tr[:, 0:6 * P].rearrange("p (c n) -> p c n", c=6), ACT.Copy).then_inc(qT_ready, 1)

                    def exps(head):
                        for second, u in enumerate(units(head)):
                            g = j * UNITS + u
                            act.wait_ge(negmax_ready, nth(l, tiles, UNITS, g))
                            if not second and head >= 3:
                                act.wait_ge(pT_mm, nth(l, tiles, HEADS, j * HEADS + head - 3))
                            if second and head - 2 >= A_HEADS:
                                act.wait_ge(mix_ready, nth(l, tiles, B_HEADS, j * B_HEADS + head - 2 - A_HEADS))
                            act.activation(w_.probs[:, probs_slot(head, second), 0:nk * P], mm(g, nk * P), ACT.Exp, bias=negmax[:, u:u + 1],
                                           scale=float(HD if u < A_HEADS else DK) ** -0.5,
                                           accum_out=rowsum[:, u:u + 1]).then_inc(exp_ready, 1)

                    def copy_probsT(head):
                        act.wait_ge(pT_mm, nth(l, tiles, HEADS, j * HEADS + head))
                        if head >= 2:
                            act.wait_ge(pv_done, nth(l, tiles, HEADS, j * HEADS + head - 2))
                        act.activation(w_.probsT[:, head % 2, 0:nk * P], tr(head, nk * P), ACT.Copy).then_inc(pT_ready, 1)

                    exps(0)
                    yield W_TILE
                    for head in range(HEADS):
                        if head:
                            copy_probsT(head - 1)
                        if head + 1 < HEADS:
                            exps(head + 1)
                        yield W_HEAD
                    copy_probsT(HEADS - 1)
                    act.wait_ge(merge_meansq, nth(l, tiles, 1, j))
                    act.activation(merge_root[:], merge_ms[:], ACT.Sqrt).then_inc(merge_rooted, 1)
                    act.wait_ge(mergedT_mm, nth(l, tiles, 1, j))
                    act.activation(hT[:, :, j * P:(j + 1) * P], ps_tr[:].rearrange("p (k n) -> p k n", k=KC),
                                   ACT.Copy).then_inc(mergedT_ready, 1)
                    yield W_TILE
                for i in range(OUT_CHUNKS * nt):
                    act.wait_ge(out_mm, nth(l, tiles, OUT_CHUNKS, i))
                    if i >= 2:
                        act.wait_ge(x_mixed, nth(l, tiles, OUT_CHUNKS, i - 2))
                    act.activation(merged[:, (i % 2) * NB:(i % 2 + 1) * NB], mm(i), ACT.Copy).then_inc(out_copied, 1)
                    yield W_OUT
                act.wait_ge(x_mixed, nth(l, tiles, OUT_CHUNKS, OUT_CHUNKS * nt - 1))
                yield from norm(l, tiles, 1)
                if tiles == P_TILES:
                    act.wait_ge(kv_stored, (l + 1) * 64)
                c = first_chunk(l, tiles) + C_KEYS
                act.wait_ge(w_full[c % WRING], (c // WRING + 1) * 16)
                act.activation(keysT.rearrange("p i n -> p (i n)"),
                               weights[:, c % WRING].rearrange("p k n -> p (k n)")[:, 0:2 * P_HEADS * P],
                               ACT.Copy).then_inc(keys_ready, 1)
                yield W_QK
                for i in range(16):
                    act.wait_ge(pq_mm, group_nth(l, tiles, i, 16))
                    if i >= 4:
                        act.wait_ge(ps_done, group_nth(l, tiles, i - 4, 16))
                    act.activation(pqT[:, i % 4, 0:nt * P], mm(i, nt * P), ACT.Copy).then_inc(pq_ready, 1)
                    yield 2 * nt

            def gate_exps(n, p):
                act.wait_ge(gate_max, n + 1)
                act.activation(pair_exp[:, p, :], pair_top[:, p, :], ACT.Exp, bias=pair_neg[:, p:p + 1],
                               accum_out=gate_sum[:, p:p + 1]).then_inc(gate_exp, 1)

            def coefficients(n, p, g, ranked):
                if g == 2 and ranked:
                    gate_exps(n + 2, p)
                part = slice(g * GROUP, (g + 1) * GROUP)
                act.wait_ge(poly_ready, n * STEPS + g + 1)
                act.activation(gexp[:, g % 2, :], poly[:, p, part], ACT.Exp, scale=-2.0 * GELU_B).then_inc(gexp_ready, 1)
                act.wait_ge(coef_ready, n * STEPS + g + 1)
                for k in range(GROUP):
                    at, slot = g * GROUP + k, (g % 2) * GROUP + k
                    act.wait_ge(v_used, n * TOPK + at + 1)
                    act.activation(diag[:, slot, :], ident, ACT.Copy, scale=coef[:, p, at:at + 1]).then_inc(diag_ready, 1)

            def copy_sum(l, t):
                act.wait_ge(acc_done, l * T + t + 1)
                act.activation(h2[:, t, :], ps_acc[:], ACT.Copy).then_inc(acc_copied, 1)

            def experts(l, tiles, side):
                n0, heads = first_head(l, tiles), len(tiles) * P_HEADS
                for h in range(heads):
                    for g in range(STEPS):
                        if h == heads - 1 and g == 2:
                            side.end()
                            side = idle
                        side.step()
                        if h == heads - 1 and g >= 2:
                            gate_exps(n0 + heads + g - 2, g - 2)
                        coefficients(n0 + h, h % 2, g, h + 2 < heads)
                    if h % P_HEADS == P_HEADS - 1:
                        copy_sum(l, tiles[h // P_HEADS])

            idle = nothing()
            for _ in modulate(0):
                pass
            for _ in dense_stages(0, P_TILES):
                pass
            gate_exps(0, 0)
            gate_exps(1, 1)
            for l in range(DEPTH):
                experts(l, P_TILES, Beside(dense_stages(l, S_TILES), dense_weight(S_TILES), P_HEADS * STEPS))
                if l + 1 < DEPTH:
                    def next_layer():
                        yield from modulate(l + 1)
                        yield from dense_stages(l + 1, P_TILES)
                    experts(l, S_TILES, Beside(next_layer(), mod_weight() + dense_weight(P_TILES), NEXT_STEPS))
            l = DEPTH - 1
            for t in S_TILES:
                n0, last = l * NH + t * P_HEADS, t == T - 1
                with act.Fori(0, P_HEADS // 2 - last) as i:
                    for p in range(2):
                        for g in range(STEPS):
                            coefficients(n0 + p + i * 2, p, g, True)
                if last:
                    for p in range(2):
                        for g in range(STEPS):
                            coefficients(n0 + P_HEADS - 2 + p, p, g, False)
                copy_sum(l, t)

        @block.vector
        def _(dve):
            step = Steps(dve, dve_step, 0, search_may)
            dve.sem_inc(u_used, URING)
            dve.wait_ge(cond_exp, 1)
            step.after(dve.tensor_scalar(cond_work[:, 1], cond_work[:, 1], 1.0, None, ALU.add))
            step.after(dve.reciprocal(cond_work[:, 1], cond_work[:, 1]))
            dve.tensor_tensor(condT[:], cond_work[:, 0], cond_work[:, 1], ALU.mult).then_inc(cond_ready, 1)

            def modulate(l):
                for n in range(ADA_CHUNKS):
                    yield W_MOD
                rows = slice(32 * l, 32 * l + ROWS)
                dve.wait_ge(mod_in_loaded, (l + 1) * 32)
                for i in range(2):
                    dve.wait_ge(mod_moved[i], (l + 1) * ADA_CHUNKS // 2 * 16)
                step.after(dve.tensor_tensor(mods[rows, :], mods[rows, :], proj_buf[rows, 0:DM], ALU.add))
                dve.scalar_tensor_tensor(out=mods[rows, :], in0=mods[rows, :], scalar=consts[rows, C_PLUS:C_PLUS + 1],
                                         in1=proj_buf[rows, DM:2 * DM], op0=ALU.add, op1=ALU.mult).then_inc(mod_ready, 1)
                yield W_QK

            def norm(l, tiles, stage):
                nt = len(tiles)
                dve.wait_ge(rms_root, group_nth(l, tiles, stage, 2))
                step.after(dve.reciprocal(rstd[:, 0:nt], rstd[:, 0:nt]))
                for j, t in enumerate(tiles):
                    i = stage * nt + j
                    h = merged[:] if stage == 0 else h2[:, t, :]
                    dve.wait_ge(gain_bc, nth(l, tiles, 2, i))
                    if stage == 0:
                        if j:
                            dve.wait_ge(h_mm, nth(l, tiles, 2, i - 1))
                        else:
                            for m in range(2):
                                dve.wait_ge(mod_moved[m], (l + 1) * ADA_CHUNKS // 2 * 16)
                    step.after(dve.scalar_tensor_tensor(out=h, in0=x[:, t, :], scalar=rstd[:, j:j + 1], in1=ps_mb[:],
                                                        op0=ALU.mult, op1=ALU.mult))
                    dve.wait_ge(shift_bc, nth(l, tiles, 2, i))
                    dve.tensor_tensor(h, h, ps_mm[:], ALU.add).then_inc(h_ready, 1)
                    yield W_NORM

            def dense_stages(l, tiles):
                w_, nt = work_of[tiles], len(tiles)
                nk = w_.slots
                neg_lam = lam_work[:, 5:6]
                yield from norm(l, tiles, 0)
                if tiles == P_TILES:
                    dve.wait_ge(params_loaded, (l + 1) * 32)
                    dve.tensor_copy(layer_base[:, l:l + 1], pcol("depth")[:, 2:3])
                    dve.tensor_tensor_reduce(scratch[:, 0:DK], pcol("lam_q1"), pcol("lam_k1"), 1.0, 0.0, ALU.mult, ALU.add,
                                             lam_work[:, 0:1])
                    step.after(dve.tensor_tensor_reduce(scratch[:, DK:2 * DK], pcol("lam_q2"), pcol("lam_k2"), 1.0, 0.0,
                                                        ALU.mult, ALU.add, lam_work[:, 1:2]))
                    dve.sem_inc(lam_sums, 1)
                for i in range(IN_CHUNKS * nt):
                    yield W_PROJ

                dve.wait_ge(proj_ready, nth(l, tiles, IN_CHUNKS, IN_CHUNKS * nt - 1))
                for j in range(nt):
                    step.after(dve.tensor_tensor(scratch[:], proj[:, j, 0:VB], proj[:, j, 0:VB], ALU.mult))
                    dve.tensor_reduce(qk_ms[:, j, 0:GA], scratch[:, 0:VA].rearrange("p (g d) -> p g d", d=HD), AXX, ALU.add)
                    step.after(dve.tensor_reduce(qk_ms[:, j, GA:], scratch[:, QB:VB].rearrange("p (g d) -> p g d", d=DK),
                                                 AXX, ALU.add))
                    if j < nt - 1:
                        yield W_QK
                dve.tensor_scalar(qk_ms[:, 0:nt, 0:GA], qk_ms[:, 0:nt, 0:GA], 1.0 / HD, EPS, ALU.mult, ALU.add)
                dve.tensor_scalar(qk_ms[:, 0:nt, GA:], qk_ms[:, 0:nt, GA:], 1.0 / DK, EPS, ALU.mult, ALU.add).then_inc(qk_meansq, 1)
                yield W_QK
                dve.wait_ge(qk_rooted, group_nth(l, tiles))
                step.after(dve.reciprocal(qk_root[:, 0:nt], qk_root[:, 0:nt]))
                for j, t in enumerate(tiles):
                    va = proj[:, j, 0:VA].rearrange("p (g d) -> p g d", d=HD)
                    vb = proj[:, j, QB:VB].rearrange("p (g d) -> p g d", d=DK)

                    def rowwise(v, gain):
                        return gain.unsqueeze(1).broadcast_to(v.shape)

                    dve.tensor_tensor(va, va, qk_root[:, j, 0:GA].unsqueeze(2).broadcast_to(va.shape), ALU.mult)
                    step.after(dve.tensor_tensor(vb, vb, qk_root[:, j, GA:].unsqueeze(2).broadcast_to(vb.shape), ALU.mult))
                    for v, gain in ((va[:, 0:A_HEADS], "qn_a"), (va[:, A_HEADS:], "kn_a"),
                                    (vb[:, 0:2 * B_HEADS], "qn_b"), (vb[:, 2 * B_HEADS:], "kn_b")):
                        last = dve.tensor_tensor(v, v, rowwise(v, pcol(gain)), ALU.mult)
                    step.after(last)
                    yield W_QK
                    if t == 0:
                        dve.sem_inc(kv_ready, 1)
                        yield W_QK
                    else:
                        table = dense[:, (t - 1) * ROPE_W:t * ROPE_W]
                        for v, cos, sin, d in ((va, table[:, 0:HD], table[:, HD:2 * HD], HD),
                                               (vb, table[:, 2 * HD:2 * HD + DK], table[:, 2 * HD + DK:], DK)):
                            g, q = v.shape[1], d // 4
                            turned = scratch[:, 0:g * d].rearrange("p (g d) -> p g d", d=d)
                            for axis in range(2):
                                for half in range(2):
                                    at, other = (2 * axis + half) * q, (2 * axis + 1 - half) * q
                                    last = dve.tensor_tensor(turned[:, :, at:at + q], v[:, :, other:other + q],
                                                             rowwise(v[:, :, at:at + q], sin[:, at:at + q]), ALU.mult)
                            step.after(last)
                            step.after(dve.tensor_tensor(v, v, rowwise(v, cos), ALU.mult))
                            step.after(dve.tensor_tensor(v, v, turned, ALU.add))
                            if v is va:
                                yield W_QK
                    if j == nt - 1:
                        dve.tensor_tensor(w_.conv_u, proj[:, 0:nt, CC:], proj[:, 0:nt, CI:CB], ALU.mult).then_inc(qk_ready, 1)
                        if tiles == P_TILES:
                            dve.wait_ge(lam_exps, l + 1)
                            step.after(dve.tensor_tensor(lam_work[:, 4:5], lam_work[:, 3:4], lam_work[:, 2:3], ALU.subtract))
                            step.after(dve.tensor_tensor(neg_lam, lam_work[:, 4:5], pcol("depth")[:, 0:1], ALU.subtract))
                    yield W_QK
                for j in range(nk):
                    yield W_KEYS_T

                for j, t in enumerate(tiles):
                    def maxima(head):
                        for u in units(head):
                            dve.wait_ge(score_mm, nth(l, tiles, UNITS, j * UNITS + u))
                            step.after(dve.tensor_reduce(rowmax[:, u:u + 1], mm(j * UNITS + u, nk * P), AXX, ALU.max))
                            dve.tensor_scalar(negmax[:, u:u + 1], rowmax[:, u:u + 1],
                                              -float(HD if u < A_HEADS else DK) ** -0.5, None,
                                              ALU.mult).then_inc(negmax_ready, 1)

                    def mix(head):
                        u = units(head)[0]
                        g = j * UNITS + u
                        dve.wait_ge(exp_ready, nth(l, tiles, UNITS, g + 1))
                        step.after(dve.reciprocal(rinv[:, u:u + 2], rowsum[:, u:u + 2]))
                        dve.tensor_tensor(rinv[:, u + 1:u + 2], rinv[:, u + 1:u + 2], neg_lam, ALU.mult)
                        first = w_.probs[:, probs_slot(head), 0:nk * P]
                        step.after(dve.tensor_scalar(first, first, rinv[:, u:u + 1], None, ALU.mult))
                        dve.scalar_tensor_tensor(out=first, in0=w_.probs[:, probs_slot(head, 1), 0:nk * P], scalar=rinv[:, u + 1:u + 2],
                                                 in1=first, op0=ALU.mult, op1=ALU.add).then_inc(mix_ready, 1)

                    if j:
                        dve.wait_ge(mergedT_mm, nth(l, tiles, 1, j - 1))
                    yc = merged[:, AW + BW:]
                    tap = pcol("conv_w").rearrange("p (i n) -> p i n", i=3)
                    side = scratch[:, 0:CW]
                    dve.wait_ge(conv_mm, nth(l, tiles, 1, j))
                    dve.tensor_tensor(yc, ps_mb[:, 0:CW], tap[:, 0], ALU.mult)
                    step.after(dve.tensor_tensor(side, w_.conv_u[:, j, :], tap[:, 1], ALU.mult))
                    step.after(dve.tensor_tensor(yc, yc, side, ALU.add))
                    dve.tensor_tensor(side, ps_mb[:, NB:NB + CW], tap[:, 2], ALU.mult).then_inc(conv_read, 1)
                    dve.wait_ge(conv_read, nth(l, tiles, 1, j))
                    step.after(dve.tensor_tensor(yc, yc, side, ALU.add))
                    step.after(dve.tensor_tensor(yc, yc, pcol("conv_b"), ALU.add))
                    step.after(dve.tensor_tensor(yc, yc, proj[:, j, CB:CC], ALU.mult))
                    maxima(0)
                    yield W_TILE
                    for head in range(HEADS):
                        if head >= A_HEADS:
                            mix(head)
                        if head + 1 < HEADS:
                            maxima(head + 1)
                        yield W_HEAD

                    step.after(dve.reciprocal(rinv[:, 0:A_HEADS], rowsum[:, 0:A_HEADS]))
                    dve.wait_ge(pv_done, nth(l, tiles, HEADS, (j + 1) * HEADS - 1))
                    ya = merged[:, 0:AW]
                    ya_heads = ya.rearrange("p (h d) -> p h d", d=HD)
                    yb = merged[:, AW:AW + BW]
                    yb_heads = yb.rearrange("p (h d) -> p h d", d=HD)
                    dve.tensor_tensor(ya_heads, ps_mb[:, 0:AW].rearrange("p (h d) -> p h d", d=HD),
                                      rinv[:, 0:A_HEADS].unsqueeze(2).broadcast_to(ya_heads.shape), ALU.mult)
                    step.after(dve.tensor_copy(yb, ps_mb[:, NB:NB + BW]))
                    dve.tensor_tensor_reduce(scratch[:, 0:AW], ya, ya, 1.0, 0.0, ALU.mult, ALU.add, merge_ms[:, 0:1])
                    dve.tensor_tensor_reduce(scratch[:, AW:AW + CW], yc, yc, 1.0, 0.0, ALU.mult, ALU.add, merge_ms[:, 1:2])
                    squares = scratch[:, AW + CW:AW + CW + BW]
                    step.after(dve.tensor_tensor(squares, yb, yb, ALU.mult))
                    step.after(dve.tensor_reduce(merge_ms[:, 2:8], squares.rearrange("p (h d) -> p h d", d=HD), AXX, ALU.add))
                    dve.tensor_scalar(merge_ms[:, 0:1], merge_ms[:, 0:1], 1.0 / AW, EPS, ALU.mult, ALU.add)
                    dve.tensor_scalar(merge_ms[:, 1:2], merge_ms[:, 1:2], 1.0 / CW, EPS, ALU.mult, ALU.add)
                    dve.tensor_scalar(merge_ms[:, 2:8], merge_ms[:, 2:8], 1.0 / HD, EPS, ALU.mult,
                                      ALU.add).then_inc(merge_meansq, 1)
                    dve.wait_ge(merge_rooted, nth(l, tiles, 1, j))
                    step.after(dve.reciprocal(merge_root[:], merge_root[:]))
                    dve.scalar_tensor_tensor(out=ya, in0=ya, scalar=merge_root[:, 0:1], in1=pcol("out_norm_a"),
                                             op0=ALU.mult, op1=ALU.mult)
                    dve.scalar_tensor_tensor(out=yc, in0=yc, scalar=merge_root[:, 1:2], in1=pcol("out_norm_c"),
                                             op0=ALU.mult, op1=ALU.mult)
                    step.after(dve.tensor_tensor(yb_heads, yb_heads,
                                                 merge_root[:, 2:8].unsqueeze(2).broadcast_to(yb_heads.shape), ALU.mult))
                    dve.scalar_tensor_tensor(out=yb_heads, in0=yb_heads, scalar=pcol("depth")[:, 1:2],
                                             in1=pcol("subln_g").unsqueeze(1).broadcast_to(yb_heads.shape),
                                             op0=ALU.mult, op1=ALU.mult).then_inc(merged_ready, 1)
                    yield W_TILE

                for i in range(OUT_CHUNKS * nt):
                    n, t = i // nt, tiles[i % nt]
                    dve.wait_ge(out_copied, nth(l, tiles, OUT_CHUNKS, i))
                    part = merged[:, (i % 2) * NB:(i % 2 + 1) * NB]
                    to = x[:, t, n * NB:(n + 1) * NB]
                    step.after(dve.tensor_tensor(part, part, ps_mb[:, (i % 2) * NB:(i % 2 + 1) * NB], ALU.mult))
                    dve.tensor_tensor(to, to, part, ALU.add).then_inc(x_mixed, 1)
                    yield W_OUT

                yield from norm(l, tiles, 1)
                yield W_QK

                def copy_scores(i):
                    dve.wait_ge(ps_done, group_nth(l, tiles, i, 16))
                    h, c = i // 2, i % 2
                    to = peer_scores.rearrange("p (t h) m -> p t h m", t=T)[:, tiles[0]:tiles[0] + nt, h, c * N_KEYS:(c + 1) * N_KEYS]
                    dve.tensor_copy(to, tr(i, nt * P).rearrange("p (t n) -> p t n", t=nt)).then_inc(ps_ready, 1)

                for i in range(16):
                    if i:
                        copy_scores(i - 1)
                    if i == 15:
                        copy_scores(i)
                    yield 2 * nt
                dve.wait_ge(ps_ready, group_nth(l, tiles, 15, 16))

            def route(step, n, l, where, p):
                step.before_search(dve.tensor_copy(st[:], peer_scores[:, where, :]))
                for lo, src in ((0, st), (8, st_rest)):
                    for c in range(2):
                        last = dve.max(half_top[:, c, lo:lo + 8], src[:, c * N_KEYS:(c + 1) * N_KEYS])
                    step.before_search(last)
                    for c in range(2):
                        half = src[:, c * N_KEYS:(c + 1) * N_KEYS]
                        last = dve.max_index(half_idx[:, c, lo:lo + 8], half_top[:, c, lo:lo + 8], half)
                    if lo == 0:
                        for c in range(2):
                            half = src[:, c * N_KEYS:(c + 1) * N_KEYS]
                            last = dve.match_replace(st_rest[:, c * N_KEYS:(c + 1) * N_KEYS], half_top[:, c, 0:8], half, NEG)
                    step.before_search(last)
                dve.tensor_copy(half_idx_f[:], half_idx[:])
                step.before_search(dve.tensor_tensor(cand[:], half_top[:, 0].unsqueeze(2).broadcast_to(cand.shape),
                                                     half_top[:, 1].unsqueeze(1).broadcast_to(cand.shape), ALU.add))
                flat = cand[:].rearrange("p a b -> p (a b)")
                step.before_search(dve.max(pair_top[:, p, 0:8], flat))
                dve.max_index(pair_pos[:, 0:8], pair_top[:, p, 0:8], flat)
                step.before_search(dve.match_replace(st[:], pair_top[:, p, 0:8], flat, NEG))
                step.before_search(dve.max(pair_top[:, p, 8:16], st[:]))
                dve.tensor_scalar(pair_neg[:, p:p + 1], pair_top[:, p, 0:1], -1.0, None, ALU.mult).then_inc(gate_max, 1)
                step.after(dve.max_index(pair_pos[:, 8:16], pair_top[:, p, 8:16], st[:]))
                dve.tensor_scalar(pair_ab[:, 0], pair_pos[:], 4, None, ALU.logical_shift_right)
                step.after(dve.tensor_scalar(pair_ab[:, 1], pair_pos[:], TOPK - 1, None, ALU.bitwise_and))
                step.after(dve.tensor_copy(pair_ab_f[:], pair_ab[:]))
                hit = (cand[:], st_rest[:].rearrange("p (a b) -> p a b", a=TOPK))
                for c in range(2):
                    last = dve.tensor_tensor(hit[c], iota16.unsqueeze(1).broadcast_to(cand.shape),
                                             pair_ab_f[:, c].unsqueeze(2).broadcast_to(cand.shape), ALU.is_equal)
                step.after(last)
                for c in range(2):
                    last = dve.tensor_tensor(hit[c], hit[c], half_idx_f[:, c].unsqueeze(1).broadcast_to(cand.shape), ALU.mult)
                step.after(last)
                for c in range(2):
                    last = dve.tensor_reduce(pair_key[:, c], hit[c], AXX, ALU.add)
                step.after(last)
                step.after(dve.scalar_tensor_tensor(out=idx_f[:], in0=pair_key[:, 0], scalar=float(N_KEYS), in1=pair_key[:, 1],
                                                    op0=ALU.mult, op1=ALU.add))
                dve.wait_ge(expert_taken, n + 1)
                dve.tensor_scalar(expert[:, p, :], idx_f[:], layer_base[:, l:l + 1], None, ALU.add).then_inc(expert_ready, 1)

            def expert_step(step, n, p, g, t, side):
                if g == 0:
                    dve.wait_ge(gate_exp, n + 1)
                    step.after(dve.reciprocal(gate_inv[:], gate_sum[:, p:p + 1]))
                    dve.tensor_scalar(gate[:, p, :], pair_exp[:, p, :], gate_inv[:], None, ALU.mult)
                for k in range(GROUP):
                    side.quarter()
                    slot, at = (g % 2) * GROUP + k, g * GROUP + k
                    dve.wait_ge(u_full[slot], (n * 2 + g // 2 + 1) * 16)
                    row = u_ring[:, slot, :]
                    dve.tensor_tensor_reduce(row, row, h2[:, t, :], 1.0, 0.0, ALU.mult, ALU.add,
                                             dots[:, p, at:at + 1]).then_inc(u_used, 1)
                dve.wait_ge(u_used, n * TOPK + (g + 1) * GROUP + URING)
                part = slice(g * GROUP, (g + 1) * GROUP)
                a, q, e = dots[:, p, part], poly[:, p, part], gexp[:, g % 2, :]
                step.after(dve.tensor_tensor(q, a, a, ALU.mult))
                step.after(dve.tensor_scalar(q, q, GELU_A, 1.0, ALU.mult, ALU.add))
                step.after(dve.tensor_tensor(q, q, a, ALU.mult))
                dve.tensor_scalar(q, q, -50.0, None, ALU.max).then_inc(poly_ready, 1)
                dve.tensor_tensor(weighed[:], a, gate[:, p, part], ALU.mult)
                dve.wait_ge(gexp_ready, n * STEPS + g + 1)
                step.after(dve.tensor_scalar(e, e, 1.0, None, ALU.add))
                step.after(dve.reciprocal(e, e))
                dve.tensor_tensor(coef[:, p, part], weighed[:], e, ALU.mult).then_inc(coef_ready, 1)

            def feed(step, tau):
                t = tau % T
                dve.wait_ge(gate2_bc, tau + 1)
                step.after(dve.tensor_tensor(h2[:, t, :], h2[:, t, :], ps_acc[:], ALU.mult))
                dve.tensor_tensor(x[:, t, :], x[:, t, :], h2[:, t, :], ALU.add).then_inc(x_fed, 1)

            def experts(l, tiles, side):
                n0, w0, heads = first_head(l, tiles), tiles[0] * P_HEADS, len(tiles) * P_HEADS
                for h in range(heads):
                    t = tiles[h // P_HEADS]
                    for g in range(STEPS):
                        if h % P_HEADS == 0 and g == 1 and l * T + t:
                            feed(step, l * T + t - 1)
                        if g == 2 and h + 2 < heads:
                            route(step, n0 + h + 2, l, w0 + h + 2, h % 2)
                        if h == heads - 1 and g >= 2:
                            if g == 2:
                                side.end()
                                side = idle
                            n, p = n0 + heads + g - 2, g - 2
                            route(step, n, n // NH, n % NH, p)
                        expert_step(step, n0 + h, h % 2, g, t, side)

            for _ in modulate(0):
                pass
            idle = nothing()
            for _ in dense_stages(0, P_TILES):
                pass
            for h in range(2):
                route(step, h, 0, h, h)
            for l in range(DEPTH):
                experts(l, P_TILES, Beside(dense_stages(l, S_TILES), dense_weight(S_TILES), P_HEADS * STEPS))
                if l + 1 < DEPTH:
                    def next_layer():
                        yield from modulate(l + 1)
                        yield from dense_stages(l + 1, P_TILES)
                    experts(l, S_TILES, Beside(next_layer(), mod_weight() + dense_weight(P_TILES), NEXT_STEPS))
            l = DEPTH - 1
            for t in S_TILES:
                n0, last = l * NH + t * P_HEADS, t == T - 1
                feed(step, l * T + t - 1)

                def pair(s, i, ranked=True):
                    for p in range(2):
                        for g in range(STEPS):
                            if g == 2 and ranked:
                                route(s, n0 + p + 2 + i * 2, l, t * P_HEADS + p + 2 + i * 2, p)
                            expert_step(s, n0 + p + i * 2, p, g, t, idle)

                with dve.Fori(0, P_HEADS // 2 - last) as i:
                    inner = Steps(dve, dve_step, i * PAIR_STEPS + (step.base + step.n), search_may)
                    pair(inner, i)
                    assert inner.n == PAIR_STEPS, inner.n
                step.n += (P_HEADS // 2 - last) * PAIR_STEPS
                if last:
                    pair(step, P_HEADS // 2 - 1, ranked=False)
            feed(step, DEPTH * T - 1)


PAIR_STEPS = 74
QUARTERS_BEFORE_ROW = (2, 1, 1, 0)
NEXT_STEPS = 62


def rope_tables():
    tokens = np.arange(2 * P)
    parts = []
    for dim in (HD, DK):
        quarter = dim // 4
        inv = np.float32(ROPE_BASE) ** (-np.arange(quarter, dtype=np.float32) / np.float32(quarter))
        cos, sin = [], []
        for pos in (tokens // GRID_W, tokens % GRID_W):
            angle = pos.astype(np.float32)[:, None] * inv
            cos += [np.cos(angle)] * 2
            sin += [-np.sin(angle), np.sin(angle)]
        parts += [np.concatenate(cos, 1), np.concatenate(sin, 1)]
    return np.concatenate(parts, 1).astype(np.float32)


def shape_constants():
    const = np.zeros((P, N_CONST), np.float32)
    const[:, C_ID:C_ID + P] = np.eye(P)
    const[:, C_IOTA:C_IOTA + TOPK] = np.arange(TOPK)
    const[:, C_EPS] = EPS
    for row in range(P):
        const[row, C_PLUS] = row % 32 < ROWS and row % 32 % 6 in (GAIN1, GAIN2)
    dense = np.zeros((P, N_DENSE), np.float32)
    rope = rope_tables()
    dense[:, 0:ROPE_W] = rope[0:P]
    dense[:, ROPE_W:] = rope[P:]
    depth = np.zeros((DEPTH, 4), np.float32)
    for l in range(DEPTH):
        lam_init = 0.8 - 0.6 * np.exp(-0.3 * l)
        depth[l] = lam_init, 1.0 - lam_init, l * N_EXPERTS, 0.0
    return const, dense, depth


def kernel(**inputs):
    import concourse.bacc as bacc
    from concourse.bass_utils import run_bass_kernel_spmd

    a = {k: np.ascontiguousarray(v) for k, v in inputs.items()}
    const, dense, depth = shape_constants()
    packed = {"depth": depth}
    for name in PARAMS:
        if name != "depth":
            packed[name] = a[name].reshape(DEPTH, -1)
    arrays = {n: a[n] for n in ("x_prompt", "x_sample", "cache_a_k", "cache_a_v", "cache_b_k", "cache_b_v")}
    arrays["cond"] = np.concatenate([a["c"].reshape(1, DM), a["c_ctx"].reshape(1, DM)])
    arrays["ada_w"] = a["ada_w"]
    arrays["ada_b"] = np.tile(a["ada_b"].reshape(DEPTH, 6, DM), (1, 2, 1))
    gains = np.ones((DEPTH, ROWS, DM), np.float32)
    gains[:, [GAIN1, 6 + GAIN1]] = a["norm1_g"][:, None]
    gains[:, [GAIN2, 6 + GAIN2]] = a["norm2_g"][:, None]
    arrays["norm_g"] = gains
    arrays["w_in"] = a["w_in"]
    arrays["params"] = np.concatenate([packed[n] for n in PARAMS], axis=1)
    arrays["w_out"], arrays["peer_wq"] = a["w_out"], a["peer_wq"]
    arrays["peer_keys"] = np.ascontiguousarray(a["peer_keys"].transpose(0, 4, 1, 2, 3)).reshape(DEPTH, P, -1)
    arrays["peer_u"] = a["peer_u"].reshape(DEPTH * N_EXPERTS, DM)
    arrays["peer_v"] = a["peer_v"].reshape(DEPTH * N_EXPERTS, DM)
    arrays["const"], arrays["dense_const"] = const, dense
    outs = {"y_prompt": (1, P, DM), "y_sample": (1, 2 * P, DM),
            "new_a_k": (1, DEPTH, P, A_KV, HD), "new_a_v": (1, DEPTH, P, A_KV, HD),
            "new_b_k": (1, DEPTH, P, B_HEADS, 2, DK), "new_b_v": (1, DEPTH, P, B_HEADS, HD)}
    nc = bacc.Bacc("TRN2", target_bir_lowering=False, num_devices=1)
    aps = {n: nc.dram_tensor(n, v.shape, mybir.dt.from_np(v.dtype), kind="ExternalInput").ap() for n, v in arrays.items()}
    aps |= {n: nc.dram_tensor(n, s, F32, kind="ExternalOutput").ap() for n, s in outs.items()}
    build(nc, **aps)
    r = run_bass_kernel_spmd(nc, [arrays], core_ids=[0])
    return tuple(r.results[0][n] for n in outs)
```
